# Optimizing a Trainium2 kernel written in Bass

```python
import math
import jax, jax.numpy as jnp
from jax import lax
import numpy as np

D_MODEL = 1024
BATCH = 1
SEQ = 512
DEPTH = 2

MIX_WIDTH = D_MODEL
ATTN_HEAD_DIM = 128
ATTN_HEADS = (MIX_WIDTH // 2) // ATTN_HEAD_DIM
ATTN_WIDTH = ATTN_HEADS * ATTN_HEAD_DIM
IDX_HEADS = 8
IDX_HEAD_DIM = 64
TOPK_MAX = 256
LRU_WIDTH = MIX_WIDTH - ATTN_WIDTH
LRU_BLOCKS = 8
LRU_BLOCK = LRU_WIDTH // LRU_BLOCKS
CONV_WIDTH = 4
LRU_C = 8.0
D_FF = 4 * D_MODEL
ROPE_THETA = 10000.0
Q_BLOCK = 128
LN_EPS = 1e-5
N_MOD = 6
SPLIT_SIZES = (ATTN_WIDTH, ATTN_WIDTH, ATTN_WIDTH,
               IDX_HEADS * IDX_HEAD_DIM, IDX_HEAD_DIM, IDX_HEADS,
               LRU_WIDTH, LRU_WIDTH)
IN_COLS = sum(SPLIT_SIZES)

kernel_name = "hymba_dsa_rglru_deepnorm_adaln"

def _deepnorm_alpha():
    return (2.0 * DEPTH) ** 0.25

def _deepnorm_beta():
    return (8.0 * DEPTH) ** -0.25

def layer_norm(x, g, b):
    xf = x.astype(jnp.float32)
    mu = jnp.mean(xf, -1, keepdims=True)
    var = jnp.mean(jnp.square(xf - mu), -1, keepdims=True)
    y = (xf - mu) * lax.rsqrt(var + LN_EPS) * g.astype(jnp.float32) + b.astype(jnp.float32)
    return y.astype(x.dtype)

def rms_norm(x, g):
    xf = x.astype(jnp.float32)
    y = xf * lax.rsqrt(jnp.mean(jnp.square(xf), -1, keepdims=True) + LN_EPS) * g.astype(jnp.float32)
    return y.astype(x.dtype)

def rope_tables(positions, dim):
    inv = ROPE_THETA ** (-jnp.arange(0, dim, 2, dtype=jnp.float32) / dim)
    ang = positions.astype(jnp.float32)[..., None] * inv
    return jnp.cos(ang)[:, :, None, :], jnp.sin(ang)[:, :, None, :]

def apply_rope(x, cos, sin):
    x1, x2 = jnp.split(x.astype(jnp.float32), 2, axis=-1)
    y = jnp.concatenate([x1 * cos - x2 * sin, x2 * cos + x1 * sin], axis=-1)
    return y.astype(x.dtype)

def dsa_attention(q, k, v, qi, ki, wi):
    B, L = q.shape[0], q.shape[1]
    topk = min(TOPK_MAX, L // 4)
    qb = min(Q_BLOCK, L)
    nblk = L // qb

    def to_blocks(a):
        return a.reshape((B, nblk, qb) + a.shape[2:]).swapaxes(0, 1)

    t_blocks = jnp.arange(L, dtype=jnp.int32).reshape(nblk, qb)
    key_pos = jnp.arange(L, dtype=jnp.int32)
    scale = ATTN_HEAD_DIM ** -0.5
    ki32 = ki.astype(jnp.float32)

    def block(args):
        q_b, qi_b, wi_b, t_b = args
        causal = key_pos[None, :] <= t_b[:, None]
        rel = jax.nn.relu(jnp.einsum('bthd,bsd->bths', qi_b.astype(jnp.float32), ki32))
        idx_score = jnp.einsum('bths,bth->bts', rel, wi_b.astype(jnp.float32))
        idx_score = jnp.where(causal[None], idx_score, -jnp.inf)
        _, sel = lax.top_k(idx_score, topk)
        valid = sel <= t_b[None, :, None]
        k_sel = jax.vmap(lambda kb, ib: kb[ib])(k, sel)
        v_sel = jax.vmap(lambda vb, ib: vb[ib])(v, sel)
        s = jnp.einsum('bthd,btkhd->bhtk', q_b, k_sel).astype(jnp.float32) * scale
        s = jnp.where(valid[:, None], s, -jnp.inf)
        p = jax.nn.softmax(s, axis=-1).astype(v.dtype)
        return jnp.einsum('bhtk,btkhd->bthd', p, v_sel)

    out = lax.map(block, (to_blocks(q), to_blocks(qi), to_blocks(wi), t_blocks))
    return out.swapaxes(0, 1).reshape(B, L, -1)

def causal_depthwise_conv(x, w, b):
    S = x.shape[1]
    xp = jnp.pad(x, ((0, 0), (CONV_WIDTH - 1, 0), (0, 0)))
    y = b
    for j in range(CONV_WIDTH):
        y = y + xp[:, j:j + S] * w[j]
    return y

def _lin_combine(left, right):
    a1, b1 = left
    a2, b2 = right
    return a1 * a2, a2 * b1 + b2

def rg_lru(xc, w_a, b_a, w_x, b_x, lam):
    B, S, _ = xc.shape
    xf = xc.astype(jnp.float32)
    xb = xf.reshape(B, S, LRU_BLOCKS, LRU_BLOCK)
    r = jax.nn.sigmoid(jnp.einsum('bsnc,ncd->bsnd', xb, w_a.astype(jnp.float32)).reshape(B, S, -1)
                       + b_a.astype(jnp.float32))
    i = jax.nn.sigmoid(jnp.einsum('bsnc,ncd->bsnd', xb, w_x.astype(jnp.float32)).reshape(B, S, -1)
                       + b_x.astype(jnp.float32))
    log_a = -LRU_C * r * jax.nn.softplus(-lam.astype(jnp.float32))
    a = jnp.exp(log_a)
    u = jnp.sqrt(-jnp.expm1(2.0 * log_a)) * (i * xf)
    _, h = lax.associative_scan(_lin_combine, (a, u), axis=1)
    return h.astype(xc.dtype)

def setup_inputs(seed: int = 0) -> dict:
    key = jax.random.key(seed)
    ks = jax.random.split(key, 24)
    f32 = jnp.float32
    beta = _deepnorm_beta()
    L = DEPTH

    def nrm(k, shape, std):
        return jax.random.normal(k, shape, f32) * std

    x = jax.random.normal(ks[0], (BATCH, SEQ, D_MODEL), f32)
    c = jax.random.normal(ks[1], (BATCH, D_MODEL), f32)
    positions = jnp.broadcast_to(jnp.arange(SEQ, dtype=jnp.int32)[None, :], (BATCH, SEQ))

    w_mod = nrm(ks[2], (L, D_MODEL, N_MOD * D_MODEL), 0.1 * D_MODEL ** -0.5)
    b_mod = nrm(ks[3], (L, N_MOD * D_MODEL), 0.01)

    col_scale = np.ones((IN_COLS,), np.float32)
    col_scale[2 * ATTN_WIDTH:3 * ATTN_WIDTH] = beta
    w_in = nrm(ks[4], (L, D_MODEL, IN_COLS), D_MODEL ** -0.5) * jnp.asarray(col_scale)

    conv_w = nrm(ks[5], (L, CONV_WIDTH, LRU_WIDTH), CONV_WIDTH ** -0.5)
    conv_b = nrm(ks[6], (L, LRU_WIDTH), 0.01)
    w_gate_a = nrm(ks[7], (L, LRU_BLOCKS, LRU_BLOCK, LRU_BLOCK), LRU_BLOCK ** -0.5)
    b_gate_a = nrm(ks[8], (L, LRU_WIDTH), 0.01)
    w_gate_x = nrm(ks[9], (L, LRU_BLOCKS, LRU_BLOCK, LRU_BLOCK), LRU_BLOCK ** -0.5)
    b_gate_x = nrm(ks[10], (L, LRU_WIDTH), 0.01)
    u = jax.random.uniform(ks[11], (L, LRU_WIDTH), f32, 0.9, 0.999)
    a0 = u ** (1.0 / LRU_C)
    lru_lambda = jnp.log(a0) - jnp.log1p(-a0)

    g_attn_out = 1.0 + nrm(ks[12], (L, ATTN_WIDTH), 0.02)
    g_lru_out = 1.0 + nrm(ks[13], (L, LRU_WIDTH), 0.02)
    w_out = nrm(ks[14], (L, MIX_WIDTH, D_MODEL), MIX_WIDTH ** -0.5 * beta)
    ln1_g = 1.0 + nrm(ks[15], (L, D_MODEL), 0.02)
    ln1_b = nrm(ks[16], (L, D_MODEL), 0.02)
    w_up = nrm(ks[17], (L, D_MODEL, D_FF), D_MODEL ** -0.5)
    w_down = nrm(ks[18], (L, D_FF, D_MODEL), D_FF ** -0.5 * beta)
    ln2_g = 1.0 + nrm(ks[19], (L, D_MODEL), 0.02)
    ln2_b = nrm(ks[20], (L, D_MODEL), 0.02)

    return {"x": x, "c": c, "positions": positions,
            "w_mod": w_mod, "b_mod": b_mod, "w_in": w_in,
            "conv_w": conv_w, "conv_b": conv_b,
            "w_gate_a": w_gate_a, "b_gate_a": b_gate_a,
            "w_gate_x": w_gate_x, "b_gate_x": b_gate_x, "lru_lambda": lru_lambda,
            "g_attn_out": g_attn_out, "g_lru_out": g_lru_out, "w_out": w_out,
            "ln1_g": ln1_g, "ln1_b": ln1_b, "w_up": w_up, "w_down": w_down,
            "ln2_g": ln2_g, "ln2_b": ln2_b}

def reference(x, c, positions, w_mod, b_mod, w_in, conv_w, conv_b, w_gate_a, b_gate_a,
              w_gate_x, b_gate_x, lru_lambda, g_attn_out, g_lru_out, w_out,
              ln1_g, ln1_b, w_up, w_down, ln2_g, ln2_b):
    B, S, _ = x.shape
    alpha = _deepnorm_alpha()
    split_at = [int(v) for v in np.cumsum(SPLIT_SIZES)[:-1]]
    cos_a, sin_a = rope_tables(positions, ATTN_HEAD_DIM)
    cos_i, sin_i = rope_tables(positions, IDX_HEAD_DIM)
    c_act = jax.nn.silu(c)

    for l in range(DEPTH):
        mod = (c_act @ w_mod[l] + b_mod[l])[:, None, :]
        sh1, sc1, g1, sh2, sc2, g2 = jnp.split(mod, N_MOD, axis=-1)

        h = x * (1.0 + sc1) + sh1
        p = h @ w_in[l]
        q, k, v, qi, ki, wi, xr, yg = jnp.split(p, split_at, axis=-1)
        q = apply_rope(q.reshape(B, S, ATTN_HEADS, ATTN_HEAD_DIM), cos_a, sin_a)
        k = apply_rope(k.reshape(B, S, ATTN_HEADS, ATTN_HEAD_DIM), cos_a, sin_a)
        v = v.reshape(B, S, ATTN_HEADS, ATTN_HEAD_DIM)
        qi = apply_rope(qi.reshape(B, S, IDX_HEADS, IDX_HEAD_DIM), cos_i, sin_i)
        ki = apply_rope(ki[:, :, None, :], cos_i, sin_i)[:, :, 0, :]
        wi = wi * (IDX_HEADS ** -0.5)
        attn_out = dsa_attention(q, k, v, qi, ki, wi)

        xc = causal_depthwise_conv(xr, conv_w[l], conv_b[l])
        lru_out = rg_lru(xc, w_gate_a[l], b_gate_a[l], w_gate_x[l], b_gate_x[l], lru_lambda[l])
        lru_out = lru_out * jax.nn.gelu(yg, approximate=True)

        merged = jnp.concatenate([rms_norm(attn_out, g_attn_out[l]),
                                  rms_norm(lru_out, g_lru_out[l])], axis=-1)
        mix = merged @ w_out[l]
        x = layer_norm(alpha * x + (1.0 + g1) * mix, ln1_g[l], ln1_b[l])

        h2 = x * (1.0 + sc2) + sh2
        ff = jnp.square(jax.nn.relu(h2 @ w_up[l])) @ w_down[l]
        x = layer_norm(alpha * x + (1.0 + g2) * ff, ln2_g[l], ln2_b[l])
    return x


_drawn_inputs = setup_inputs


def setup_inputs(seed=0):
    import zlib

    import numpy as np

    out = dict(_drawn_inputs(seed))
    spreads = {}
    factors = {'b_gate_a': 8.0, 'b_gate_x': 8.0, 'g_attn_out': 5.32, 'g_lru_out': 5.283}
    for name, (base, spread) in spreads.items():
        noise = np.random.default_rng([zlib.crc32(name.encode()), seed]).standard_normal(out[name].shape)
        drawn = base * np.exp(spread * noise) if base else spread * noise
        out[name] = __import__('jax').numpy.asarray(drawn.astype(out[name].dtype))
    for name, factor in factors.items():
        out[name] = (out[name] * factor).astype(out[name].dtype)
    return out
```

```python
import numpy as np

import concourse.bass as bass
from concourse import mybir
from contextlib import ExitStack

F32 = mybir.dt.float32
F32R = mybir.dt.float32r
I32 = mybir.dt.int32
ALU = mybir.AluOpType
ACT = mybir.ActivationFunctionType
AX_X = mybir.AxisListType.X

P = 128
DEPTH, D, T, DFF = 2, 1024, 512, 4096
DK = D // P
TT = T // P
HEADS, DH = 4, 128
IDX_HEADS, IDX_DH = 8, 64
TOPK = min(256, T // 4)
AW = HEADS * DH
LW = D - AW
LT = LW // P
CONV = 4
LRU_C = 8.0
LN_EPS = 1e-5
ALPHA = (2.0 * DEPTH) ** 0.25
THETA = 10000.0
SCALE = DH ** -0.5
BIG = 3.0e38
TAKEN = -3.4e38

COL = {}
_at = 0
for _name, _n in (("q", AW), ("k", AW), ("v", AW), ("qi", IDX_HEADS * IDX_DH), ("kiwi", IDX_DH + IDX_HEADS),
                  ("xr", LW), ("yg", LW)):
    COL[_name] = _at
    _at += _n
KIWI = IDX_DH + IDX_HEADS

PRE = ["qi", "xr", "yg", "v", "k", "q", "out0", "out1"]
CHUNK = ["up0", "up1", "down0", "down1"]
NC = DFF // D
PAIRS = 4
GROUPS = len(PRE) + NC * len(CHUNK)
OUT_ORDER = [4, 5, 6, 7, 0, 1, 2, 3]

VEC = {}
_at = 0
for _name, _n in (("b_mod", 6 * DK), ("conv_w", CONV * LT), ("conv_b", LT), ("b_gate_a", LT), ("b_gate_x", LT),
                  ("lru_lambda", LT), ("g_attn_out", HEADS), ("g_lru_out", LT), ("ln1_g", DK), ("ln1_b", DK),
                  ("ln2_g", DK), ("ln2_b", DK)):
    VEC[_name] = (_at, _n)
    _at += _n
NV = _at
MODS_NEXT = 2 * DK
MODS_LATE = 4 * DK

UNITS = [(i, h) for i in range(TT) for h in range(HEADS)]
IDX = [(i, h) for i in range(1, TT) for h in range(IDX_HEADS)]
_pre = {b: [n + str(b) for n in PRE[:6]] for b in range(4)}
for _b in (0, 1):
    _pre[_b] += [f"o{i}" for i in range(TT) if i % 2 == _b]
for _b in (2, 3):
    _pre[_b] += [f"pt{u}" for u in range(len(UNITS)) if u % 2 == _b - 2]
for _b in range(4):
    _pre[_b] += [f"out0{_b}"]
_pre[4] = ["kiwi", "wi"] + [f"gr{m}" for m in range(LT)] + [f"vt{m}" for m in range(HEADS)] + ["out10", "mean"]
_pre[5] = [f"idx{u}" for u in range(0, len(IDX), 2)] + [f"s{u}" for u in range(0, 16, 2)] + ["ams", "out11", "e2"]
_pre[6] = [f"idx{u}" for u in range(1, len(IDX), 2)] + [f"s{u}" for u in range(1, 16, 2)] + ["lms", "out12"]
_pre[7] = [f"gi{m}" for m in range(LT)] + ["out13"]
_chunk = {b: [f"up0{b}", f"down0{b}"] for b in range(4)}
for _b in range(4):
    _chunk[4 + _b] = [f"up1{_b}", f"down1{_b}"]
_post = {b: [] for b in range(8)}
_post[4], _post[5] = ["mean_b"], ["e2_b"]


def uses_before(b, name, l, c=None):
    per = len(_pre[b]) + NC * len(_chunk[b]) + len(_post[b])
    if c is not None:
        return l * per + c * len(_chunk[b]) + (len(_pre[b]) + _chunk[b].index(name) + 1)
    if name in _post[b]:
        return l * per + (len(_pre[b]) + NC * len(_chunk[b]) + _post[b].index(name) + 1)
    return l * per + (_pre[b].index(name) + 1)


def group_at(name, l, c=None):
    if c is None:
        return l * GROUPS + PRE.index(name)
    return l * GROUPS + c * len(CHUNK) + (len(PRE) + CHUNK.index(name))


def bank_set(name):
    return 4 if name in ("out1", "up1", "down1") else 0


ACC_AT = {1: 0, 2: 2 * P, 3: 5 * P}


def trunk_kernel(nc, A, out):
    ctx = ExitStack()
    with ctx:
        top = [(nc.sbuf_base + 63) // 64 * 64]

        def place(nbytes):
            at = top[0]
            top[0] += (nbytes + 31) // 32 * 32
            assert top[0] <= nc.sbuf_usable_end, (top[0], nc.sbuf_usable_end)
            return at

        def sb(name, shape, dt=F32, at=None):
            n = 4 * int(np.prod(shape[1:]))
            return nc.alloc_sbuf_tensor_at(name, shape, dt, offset=place(n) if at is None else at)

        K2 = 4 * T
        x = sb("resid", [P, DK, T])
        a_hi = sb("a_hi", [P, DK, T], F32R)
        a_lo = sb("a_lo", [P, DK, T], F32R)
        b_at = place(16 * K2)
        b_hi = sb("b_hi", [P, DK, T], F32R, b_at)
        b_lo = sb("b_lo", [P, DK, T], F32R, b_at + 8 * K2)
        qi = sb("qi_rot", [P, 4, T], F32, b_at)
        sq_l = sb("lru_sq", [P, LT, T], F32, b_at)
        q = sb("q_rot", [P, HEADS, T], F32, b_at + 4 * K2)
        th = sb("lru_root", [P, LT, T], F32, b_at + 4 * K2)
        k = sb("k_rot", [P, HEADS, T], F32, b_at + 8 * K2)
        gi = sb("lru_gate", [P, LT, T], F32, b_at + 8 * K2)
        v = sb("v_tok", [P, TT, AW], F32, b_at + 12 * K2)
        xs = sb("x_in", [P, TT, D], F32, b_at)
        raw = sb("w_raw", [P, PAIRS, 2, T])
        w_hi = sb("w_hi", [P, PAIRS, 2, T], F32R)
        w_lo = sb("w_lo", [P, PAIRS, 2, T], F32R)
        kiwi_at = place(4 * DK * KIWI)
        kiwi_raw = sb("kiwi_raw", [P, DK, KIWI], F32, kiwi_at)
        lru_rstd = sb("lru_rstd", [P, T], F32, kiwi_at)
        kiwi_hi = sb("kiwi_hi", [P, DK, KIWI], F32R)
        kiwi_lo = sb("kiwi_lo", [P, DK, KIWI], F32R)
        mod_raw = sb("mod_raw", [P, 2, DK, P])
        ki_a = sb("ki_even", [P, T])
        ki_b = sb("ki_odd", [P, T])
        xr_at = place(4 * LT * (T + CONV - 1))
        xr = sb("xr", [P, LT, T + CONV - 1], F32, xr_at)
        lru_a = sb("lru_a", [P, LT, T], F32, xr_at)
        probs = sb("probs", [P, 2, T], F32, xr_at)
        probs_t = sb("probs_t", [P, 2, T], F32, xr_at + 2 * K2)
        ln_sq = sb("ln_sq", [P, 2, T], F32, xr_at)
        xc_at = place(4 * K2)
        xc = sb("xc", [P, LT, T], F32, xc_at)
        mean = sb("ln_mean", [P, T], F32, xc_at)
        rstd = sb("ln_rstd", [P, T], F32, xc_at + K2)
        var = sb("ln_var", [P, T], F32, xc_at + 2 * K2)
        yg_at = place(4 * K2)
        yg = sb("gelu_gate", [P, LT, T], F32, yg_at)
        ao = sb("attn_out", [P, HEADS, T], F32, yg_at)
        ang = sb("angles", [P, 4, T], F32, yg_at)
        cos_m, sin_m, cos_i, sin_i = (sb(n, [P, T]) for n in ("cos_m", "sin_m", "cos_i", "sin_i"))
        acc_at = place(4 * 9 * P)
        acc = sb("idx_acc", [P, 9 * P], F32, acc_at)
        attn_rstd = sb("attn_rstd", [P, T], F32, acc_at)
        ln_s = sb("ln_s", [P, T], F32, acc_at)
        ln_q = sb("ln_q", [P, T], F32, acc_at + K2)
        causal = sb("causal", [P, TT * P])
        full_at = place(2 * K2)
        rel = sb("idx_rel", [P, 2, T], F32, full_at)
        full = sb("unsplit", [P, 2, T], F32, full_at)
        rope_at = place(4 * K2)
        rraw = sb("rope_raw", [P, 2, T], F32, rope_at)
        rrot = sb("rope_swapped", [P, 2, T], F32, rope_at + 2 * K2)
        relu = sb("ff_relu", [P, 2, T], F32, rope_at)
        ffsq = sb("ff_square", [P, 2, T], F32, rope_at + 2 * K2)
        sq_a = sb("attn_sq", [P, TT, T], F32, rope_at)
        pos = sb("positions_b", [P, T], I32, rope_at)
        turns_i = sb("turns_i", [P, T], I32, rope_at + K2)
        posf = sb("positions_f", [P, T], F32, rope_at + 2 * K2)
        stage = sb("vec_rows", [P, DEPTH, P], F32, full_at)
        blk = sb("gate_blocks", [P, 2, LT, P])
        vecs = sb("vecs", [P, DEPTH, P])
        vec = sb("vec", [P, NV])
        ident = sb("ident", [P, P])
        ones_d = sb("ones_d", [P, P])
        csil = sb("csil", [P, DK])
        mods = sb("mods", [P, 6 * DK])
        modn = sb("modn", [P, MODS_NEXT])
        gains = sb("gains", [P, 8, DK])
        small = sb("small", [P, 4, 16])
        wi = sb("wi", [P, TT, IDX_HEADS])
        best = sb("best", [P, 8])
        eps = sb("eps", [P, 1])
        neg_sp = sb("neg_sp", [P, LT])
        freq = sb("freq", [P, 2])
        spt = sb("spt", [P, 4, DEPTH, LT])
        mx, negm, rsum, rinv = (small[:, n, :] for n in range(4))

        banks = [ctx.enter_context(nc.psum_tensor(f"bank{b}", [P, T], F32)) for b in range(8)]

        def sem(name):
            return ctx.enter_context(nc.semaphore(name))

        full_s = [sem(f"bank_full{b}") for b in range(8)]
        free_s = [sem(f"bank_free{b}") for b in range(8)]
        raw_in = [sem(f"raw_in{s}") for s in range(PAIRS)]
        kiwi_in, kiwi_hi_s, kiwi_lo_s = sem("kiwi_in"), sem("kiwi_hi_done"), sem("kiwi_lo_done")
        hi_split, lo_split = sem("hi_split"), sem("lo_split")
        pair_used = sem("pair_used")
        mod_in = [sem("mod_in0"), sem("mod_in1")]
        mods_out = sem("mods_out")
        mod_used = sem("mod_used")
        gate_in = sem("gate_in")
        xn_ready = sem("xn_ready")
        a_hi_s, a_lo_s = sem("a_hi_done"), sem("a_lo_done")
        x_scaled = sem("x_scaled")
        m_full, b_hi_s, b_lo_s = sem("merged_full"), sem("b_hi_done"), sem("b_lo_done")
        ff_sq = sem("ff_squared")
        rope_done = sem("rope_done")
        idx_acc = sem("idx_accumulated")
        conv_done, lru_exp, lru_m, lru_sqrt, lru_out = (sem(n) for n in ("conv_done", "lru_exp", "lru_m", "lru_sqrt", "lru_out"))
        attn_max, attn_exp, attn_p = sem("attn_max"), sem("attn_exp"), sem("attn_p")
        pv_done = sem("pv_done")
        sq_ready = sem("squares_ready")
        ln_sq_s, ln_q_s, ln_s_s = sem("ln_squared"), sem("ln_q_added"), sem("ln_s_added")
        ln_var, ln_std = sem("ln_var"), sem("ln_std")
        loads_begun, wi_begun = sem("loads_begun"), sem("wi_begun")
        gains_ready, vec_ready = sem("gains_ready"), sem("vec_ready")
        dve_step = sem("dve_step")
        p_in_small, p_in_x, p_in_pos, p_const = sem("p_in_small"), sem("p_in_x"), sem("p_in_pos"), sem("p_const")
        p_pe, p_act, p_dve = sem("p_pe"), sem("p_act"), sem("p_dve")
        p_ang, p_sin = sem("p_angles"), sem("p_sines")
        y_ready, y_t, y_out, stored = sem("y_ready"), sem("y_turned"), sem("y_out"), sem("stored")

        class Chain:

            def __init__(self, eng, s):
                self.eng, self.s, self.n = eng, s, 0

            def __call__(self, ins):
                ins.then_inc(self.s, 1)
                self.n += 1

            def settle(self):
                if self.n:
                    self.eng.wait_ge(self.s, self.n)

            def restart(self):
                self.settle()
                if self.n:
                    self.eng.sem_clear(self.s)
                self.n = 0

        def layers(eng, body):
            with eng.Fori(0, DEPTH) as l:
                body(l)

        def chunks(eng, l, body):
            with eng.Fori(0, NC - 1) as c:
                body(l, c, False)
            body(l, NC - 1, True)

        def vcol(name, j=0, n=1, src=vec):
            at, _ = VEC[name]
            return vec[:, at + j:at + j + n]

        def acc_of(i, n=None):
            return acc[:, ACC_AT[i]:ACC_AT[i] + (i + 1) * P]

        def bias_of(i):
            return causal[:, (TT - 1) * P:] if i == 0 else acc_of(i)

        def pair_views(name, p):
            if name != "qi":
                return [(raw[:, p, :, :], w_hi[:, p, :, :], w_lo[:, p, :, :])]
            pieces = []
            for s in range(2):
                for head in range(2):
                    src = raw[:, p, s, :].rearrange("p (m head half d) -> p head m half d", m=4, head=2, half=2)[:, head]
                    hi, lo = (w[:, p, s, :].rearrange("p (m half head d) -> p head m half d", m=4, head=2, half=2)[:, head]
                              for w in (w_hi, w_lo))
                    pieces.append((src, hi, lo))
            return pieces

        block = ctx.enter_context(nc.Block())

        @block.sync
        def _(sp):
            for n in range(TT):
                sp.dma_start(xs[:, n, :], A["x"][0, n * P:(n + 1) * P, :]).then_inc(p_in_x, 16)

            def load_pair(src, l, name, p, c=None):
                g = group_at(name, l, c)
                sp.wait_ge(lo_split, g * PAIRS + (p + 1))
                sp.sem_inc(loads_begun, 1)
                sp.dma_start(raw[:, p, :, :], src).then_inc(raw_in[p], 16)

            def layer(l):
                sp.wait_ge(m_full, l * DK + 1)
                sp.sem_inc(loads_begun, 1)
                sp.dma_start(kiwi_raw[:, :, :], A["w_in"][l, :, COL["kiwi"]:COL["kiwi"] + KIWI]
                             .rearrange("(k p) n -> p k n", p=P)).then_inc(kiwi_in, 16)
                for name in PRE[:6]:
                    for p in range(PAIRS):
                        load_pair(A["w_in"][l, 2 * p * P:(2 * p + 2) * P, COL[name]:COL[name] + T]
                                  .rearrange("(k p) n -> p k n", p=P), l, name, p)
                for j, name in enumerate(PRE[6:]):
                    for p in range(PAIRS):
                        row = OUT_ORDER[2 * p] * P
                        load_pair(A["w_out"][l, row:row + 2 * P, j * T:(j + 1) * T]
                                  .rearrange("(k p) n -> p k n", p=P), l, name, p)

                def chunk(l, c, last):
                    for j in range(2):
                        for p in range(PAIRS):
                            load_pair(A["w_up"][l, 2 * p * P:(2 * p + 2) * P, bass.ds(c * D + j * T, T)]
                                      .rearrange("(k p) n -> p k n", p=P), l, f"up{j}", p, c)
                    for j in range(2):
                        for p in range(PAIRS):
                            load_pair(A["w_down"][l, bass.ds(c * D + 2 * p * P, 2 * P), j * T:(j + 1) * T]
                                      .rearrange("(k p) n -> p k n", p=P), l, f"down{j}", p, c)
                chunks(sp, l, chunk)
            layers(sp, layer)
            for n in range(TT):
                sp.wait_ge(y_out, 2 * (n + 1))
                sp.dma_start(out[0, n * P:(n + 1) * P, :], xs[:, n, :]).then_inc(stored, 16)
            sp.wait_ge(stored, 16 * TT)

        @block.gpsimd
        def _(pool):
            gp = nc.gpsimd
            for name, (at, n) in VEC.items():
                src = A[name]
                if name == "conv_w":
                    src = src.rearrange("l j (t p) -> (j t) l p", p=P)
                else:
                    src = src.rearrange("l (t p) -> t l p", p=P)
                pool.dma_start(stage[at:at + n, :, :], src).then_inc(p_in_small, 16)
            pool.dma_start(stage[NV:P, 0, :], A["c"].rearrange("b (t p) -> (b t) p", p=P)).then_inc(p_in_small, 16)
            pool.dma_start(pos[:, :], A["positions"][0:1, :].broadcast_to([P, T])).then_inc(p_in_pos, 16)
            pool.dma_start(freq[:, :], A["freq"]).then_inc(p_in_pos, 16)
            gp.memset(ident[:, :], 0.0).then_inc(p_const, 1)
            gp.memset(causal[:, :], 0.0).then_inc(p_const, 1)
            pool.wait_ge(p_const, 2)
            gp.affine_select(out=ident[:, :], in_=ident[:, :], compare_op=ALU.not_equal, fill=1.0, base=0,
                             pattern=[[-1, P]], channel_multiplier=1).then_inc(p_const, 1)
            diag = causal[:, (TT - 1) * P:]
            gp.affine_select(out=diag, in_=diag, compare_op=ALU.is_ge, fill=-BIG, base=0,
                             pattern=[[-1, P]], channel_multiplier=1).then_inc(p_const, 1)
            gp.memset(ones_d[:, :], 1.0 / D).then_inc(p_const, 1)
            gp.memset(blk[:, :, :, :], 0.0).then_inc(p_const, 1)
            gp.memset(ki_a[:, :], 0.0).then_inc(p_const, 1)
            gp.memset(ki_b[:, :], 0.0).then_inc(p_const, 1)
            gp.memset(eps[:, :], LN_EPS).then_inc(p_const, 1)

            def load_mod(l_src, tile, count):
                pool.wait_ge(mod_used, count + 1)
                pool.dma_start(mod_raw[:, tile % 2, :, :], A["w_mod"][l_src, :, bass.ds(tile * P, P)]
                               .rearrange("(k p) n -> p k n", p=P)).then_inc(mod_in[tile % 2], 16)

            for n in range(MODS_NEXT):
                load_mod(0, n, n)
            pool.wait_ge(p_const, 9)

            def layer(l):
                base = MODS_NEXT + l * (6 * DK)
                pool.wait_ge(full_s[7], uses_before(7, "gi0", l))
                for g, name in enumerate(("w_gate_a", "w_gate_x")):
                    for par in range(2):
                        pool.dma_start(blk[64 * par:64 * par + 64, g, :, 64 * par:64 * par + 64],
                                       A[name][l, :, :, :].rearrange("(t two) c d -> two c t d", two=2)[par])\
                            .then_inc(gate_in, 16)
                for n in range(MODS_LATE):
                    load_mod(l, MODS_NEXT + n, base + n)

                def sums(at):
                    for m in range(1, DK):
                        pool.wait_ge(ln_sq_s, at * DK + (m + 1))
                        if m > 1:
                            pool.wait_ge(ln_q_s, at * (DK - 1) + (1 + m))
                        gp.tensor_tensor(ln_q[:, :], ln_q[:, :], ln_sq[:, m % 2, :], ALU.add).then_inc(ln_q_s, 1)
                sums(l * 2)

                def chunk(l, c, last):
                    for n in range(4):
                        tile = 4 * c + n
                        pool.wait_ge(mod_used, (base + MODS_LATE) + (c * 4 + (n + 1)))
                        pool.dma_start(mod_raw[:, n % 2, :, :], A["w_mod"][(l + 1) % DEPTH, :, bass.ds(tile * P, P)]
                                       .rearrange("(k p) n -> p k n", p=P)).then_inc(mod_in[n % 2], 16)
                chunks(pool, l, chunk)
                sums(l * 2 + 1)
            layers(pool, layer)

        @block.tensor
        def _(pe):
            mm = nc.tensor.matmul

            def turn(dst, src, idn):
                return nc.tensor.transpose(dst, src, idn)

            pe.wait_ge(p_const, 3)
            pe.wait_ge(p_in_small, 16 * (len(VEC) + 1))
            turn(banks[4][:, 0:P], stage[:, 0, :], ident[:, :])
            for l in range(1, DEPTH):
                last = turn(banks[4][:, l * P:l * P + NV], stage[0:NV, l, :], ident[0:NV, 0:NV])
            last.then_inc(p_pe, 1)
            pe.wait_ge(p_in_x, 16 * TT)
            for m in range(DK):
                if m >= 4:
                    pe.wait_ge(p_act, m - 4 + 2)
                for n in range(TT):
                    last = turn(banks[m % 4][:, n * P:(n + 1) * P], xs[:, n, m * P:(m + 1) * P], ident[:, :])
                last.then_inc(p_pe, 1)

            def mod_tile(col, slot, loaded, bank):
                pe.wait_ge(mod_in[slot], loaded)
                for kk in range(DK):
                    last = mm(bank[:, col:col + 1], mod_raw[:, slot, kk, :], csil[:, kk:kk + 1],
                              start=(kk == 0), stop=(kk == DK - 1))
                last.then_inc(mod_used, 1)

            pe.wait_ge(p_dve, 1)
            for n in range(MODS_NEXT):
                mod_tile(n, n % 2, 16 * (n // 2 + 1), banks[7])

            def group(name, l, hi, lo, ready, c=None, order=range(DK)):
                set_ = bank_set(name)
                g = group_at(name, l, c)
                key = name if c is None else name
                for p in range(PAIRS):
                    pe.wait_ge(lo_split, g * PAIRS + (PAIRS + p + 1))
                    steps = [(s, m) for s in range(2) for m in range(4)] if p < PAIRS - 1 else \
                        [(s, m) for m in range(4) for s in range(2)]
                    for s, m in steps:
                        kk = order[2 * p + s]
                        if m == 0:
                            ready(kk, 2 * p + s)
                        if p == 0 and s == 0:
                            pe.wait_ge(free_s[set_ + m], uses_before(set_ + m, f"{name}{m}", l, c))
                        wh, wl = (w[:, p, s, m * P:(m + 1) * P] for w in (w_hi, w_lo))
                        o = banks[set_ + m][:, :]
                        first, fin = p == 0 and s == 0, p == PAIRS - 1 and s == 1
                        mm(o, wh, hi[:, kk, :], start=first, stop=False)
                        mm(o, wh, lo[:, kk, :], start=False, stop=False)
                        last = mm(o, wl, hi[:, kk, :], start=False, stop=fin)
                        if fin:
                            last.then_inc(full_s[set_ + m], 1)
                    if p < PAIRS - 1:
                        last.then_inc(pair_used, 1)

            def a_ready(base):
                def wait(kk, n):
                    pe.wait_ge(a_lo_s, base + (2 + kk + 1))
                return wait

            def nothing(kk, n):
                pass

            def b_ready(base):
                def wait(kk, n):
                    pe.wait_ge(b_lo_s, base + (n + 1))
                return wait

            def idx_scores(i, l):
                for h in range(IDX_HEADS):
                    u = IDX.index((i, h))
                    b = 5 + u % 2
                    pe.wait_ge(rope_done, l * 13 + 5)
                    pe.wait_ge(free_s[b], uses_before(b, f"idx{u}", l))
                    mm(banks[b][:, 0:(i + 1) * P], qi[:, h // 2, i * P:(i + 1) * P],
                       (ki_b if h % 2 else ki_a)[:, 0:(i + 1) * P], start=True, stop=True).then_inc(full_s[b], 1)

            def norm_sums(l, mean_name, e2_name, n):
                pe.wait_ge(ln_s_s, n)
                pe.wait_ge(free_s[4], uses_before(4, mean_name, l))
                mm(banks[4][:, :], ones_d[:, :], ln_s[:, :], start=True, stop=True).then_inc(full_s[4], 1)
                pe.wait_ge(ln_q_s, n * (DK - 1) + 2)
                pe.wait_ge(free_s[5], uses_before(5, e2_name, l))
                mm(banks[5][:, :], ones_d[:, :], ln_q[:, :], start=True, stop=True).then_inc(full_s[5], 1)

            def layer(l):
                group("qi", l, a_hi, a_lo, a_ready(l * 2 * DK))
                pe.wait_ge(kiwi_lo_s, l + 2)
                pe.wait_ge(free_s[4], uses_before(4, "kiwi", l))
                for kk in range(DK):
                    o = banks[4][0:KIWI, :]
                    mm(o, kiwi_hi[:, kk, :], a_hi[:, kk, :], start=(kk == 0), stop=False)
                    mm(o, kiwi_hi[:, kk, :], a_lo[:, kk, :], start=False, stop=False)
                    last = mm(o, kiwi_lo[:, kk, :], a_hi[:, kk, :], start=False, stop=(kk == DK - 1))
                last.then_inc(full_s[4], 1)
                group("xr", l, a_hi, a_lo, nothing)
                pe.wait_ge(free_s[4], uses_before(4, "kiwi", l) + 1)
                pe.wait_ge(free_s[4], uses_before(4, "wi", l))
                pe.sem_inc(wi_begun, 1)
                for n in range(TT):
                    last = turn(banks[4][:, n * IDX_HEADS:(n + 1) * IDX_HEADS], rraw[64:64 + IDX_HEADS, 0, n * P:(n + 1) * P],
                                ident[64:64 + IDX_HEADS, 64:64 + IDX_HEADS])
                last.then_inc(full_s[4], 1)
                idx_scores(1, l)
                group("yg", l, a_hi, a_lo, nothing)
                idx_scores(2, l)
                pe.wait_ge(gate_in, l * 64 + 64)
                for m in range(LT):
                    pe.wait_ge(conv_done, l * LT + (m + 1))
                    for g, (b, name) in enumerate(((4, f"gr{m}"), (7, f"gi{m}"))):
                        pe.wait_ge(free_s[b], uses_before(b, name, l))
                        mm(banks[b][:, :], blk[:, g, m, :], xc[:, m, :], start=True, stop=True).then_inc(full_s[b], 1)
                group("v", l, a_hi, a_lo, nothing)
                idx_scores(3, l)
                for m in range(HEADS):
                    pe.wait_ge(free_s[m], uses_before(m, f"v{m}", l) + 1)
                    pe.wait_ge(free_s[4], uses_before(4, f"vt{m}", l))
                    for n in range(TT):
                        last = turn(banks[4][:, n * P:(n + 1) * P], rraw[:, (5 + m) % 2, n * P:(n + 1) * P], ident[:, :])
                    last.then_inc(full_s[4], 1)
                group("k", l, a_hi, a_lo, nothing)
                group("q", l, a_hi, a_lo, nothing)

                base = MODS_NEXT + l * (6 * DK)

                def scores(u):
                    i, h = UNITS[u]
                    b = 5 + u % 2
                    pe.wait_ge(free_s[b], uses_before(b, f"s{u}", l))
                    mm(banks[b][:, 0:(i + 1) * P], q[:, h, i * P:(i + 1) * P], k[:, h, 0:(i + 1) * P],
                       start=True, stop=True).then_inc(full_s[b], 1)

                def turned(u):
                    i, h = UNITS[u]
                    b = 2 + u % 2
                    pe.wait_ge(attn_p, l * 16 + (u + 1))
                    pe.wait_ge(free_s[b], uses_before(b, f"pt{u}", l))
                    for j in range(i + 1):
                        last = turn(banks[b][:, j * P:(j + 1) * P], probs[:, u % 2, j * P:(j + 1) * P], ident[:, :])
                    last.then_inc(full_s[b], 1)

                def values(u):
                    i, h = UNITS[u]
                    b = i % 2
                    pe.wait_ge(free_s[2 + u % 2], uses_before(2 + u % 2, f"pt{u}", l) + 1)
                    if h == 0:
                        pe.wait_ge(free_s[b], uses_before(b, f"o{i}", l))
                    for j in range(i + 1):
                        last = mm(banks[b][:, h * P:(h + 1) * P], v[:, j, h * DH:(h + 1) * DH],
                                  probs_t[:, u % 2, j * P:(j + 1) * P], start=(j == 0), stop=(j == i))
                    last.then_inc(full_s[b] if h == HEADS - 1 else pv_done, 1)

                def attn_squares(i):
                    pe.wait_ge(free_s[i % 2], uses_before(i % 2, f"o{i}", l) + 1)
                    if i == 0:
                        pe.wait_ge(free_s[5], uses_before(5, "ams", l))
                    for h in range(HEADS):
                        last = mm(banks[5][:, i * P:(i + 1) * P], ones_d[:, :], sq_a[:, i, h * P:(h + 1) * P],
                                  start=(h == 0), stop=(h == HEADS - 1))
                    if i == TT - 1:
                        last.then_inc(full_s[5], 1)

                def late_mod(n):
                    mod_tile(n, n % 2, l * (16 * 3 * DK) + 16 * (DK + n // 2 + 1), banks[7])

                pe.wait_ge(free_s[7], uses_before(7, "out13", l))
                for n in range(16):
                    late_mod(n)
                pe.wait_ge(rope_done, l * 13 + 13)
                pe.wait_ge(free_s[4], uses_before(4, f"vt{HEADS - 1}", l) + 1)
                scores(0)
                for u in range(len(UNITS)):
                    if u + 1 < len(UNITS):
                        scores(u + 1)
                    late_mod(16 + u)
                    turned(u)
                    if u >= 1:
                        values(u - 1)
                values(len(UNITS) - 1)
                pe.wait_ge(sq_ready, l * LT + LT)
                pe.wait_ge(free_s[6], uses_before(6, "lms", l))
                for m in range(LT):
                    last = mm(banks[6][:, :], ones_d[:, :], sq_l[:, m, :], start=(m == 0), stop=(m == LT - 1))
                last.then_inc(full_s[6], 1)
                for i in range(TT):
                    attn_squares(i)

                group("out0", l, b_hi, b_lo, b_ready(l * (5 * DK)), order=OUT_ORDER)
                pe.wait_ge(mods_out, l * (NC + 1) + 1)
                group("out1", l, b_hi, b_lo, nothing, order=OUT_ORDER)
                norm_sums(l, "mean", "e2", l * 2 + 1)

                def chunk(l, c, last):
                    group("up0", l, a_hi, a_lo, a_ready(l * 2 * DK + DK), c)
                    group("up1", l, a_hi, a_lo, nothing, c)
                    group("down0", l, b_hi, b_lo, b_ready(l * (5 * DK) + DK + c * DK), c)
                    pe.wait_ge(free_s[4], uses_before(4, "down10", l, c))
                    for n in range(4):
                        mod_tile(n, n % 2, l * (16 * 3 * DK) + 16 * (3 * DK + n // 2 + 1) + c * 32, banks[4])
                    pe.wait_ge(mods_out, l * (NC + 1) + c + 2)
                    group("down1", l, b_hi, b_lo, nothing, c)
                chunks(pe, l, chunk)
                norm_sums(l, "mean_b", "e2_b", l * 2 + 2)
            layers(pe, layer)

            for n in range(TT):
                for half in range(2):
                    b = 2 * (n % 2) + half
                    if n >= 2:
                        pe.wait_ge(y_out, 2 * (n - 2) + half + 1)
                    for m in range(4):
                        if n == 0:
                            pe.wait_ge(y_ready, 4 * half + m + 1)
                        last = turn(banks[b][:, m * P:(m + 1) * P], x[:, 4 * half + m, n * P:(n + 1) * P], ident[:, :])
                    last.then_inc(y_t, 1)

        @block.scalar
        def _(act):
            af = nc.scalar.activation

            act.wait_ge(p_pe, 1)
            for l in range(DEPTH):
                n = P if l == 0 else NV
                last = af(vecs[:, l, 0:n], banks[4][:, l * P:l * P + n], ACT.Copy)
            last.then_inc(p_act, 1)
            act.wait_ge(p_act, 1)
            af(csil[:, :], vecs[:, 0, NV:P], ACT.Sigmoid).then_inc(p_sin, 1)
            at, n = VEC["lru_lambda"]
            af(spt[:, 0, :, :], vecs[:, :, at:at + n], ACT.Abs).then_inc(p_sin, 1)
            act.wait_ge(p_sin, 2)
            af(spt[:, 0, :, :], spt[:, 0, :, :], ACT.Exp, scale=-1.0).then_inc(p_sin, 1)
            for m in range(DK):
                act.wait_ge(p_pe, m + 2)
                af(x[:, m, :], banks[m % 4][:, :], ACT.Copy).then_inc(p_act, 1)
            act.wait_ge(p_ang, 1)
            for dst, src in ((sin_m, 0), (sin_i, 1), (cos_m, 2), (cos_i, 3)):
                af(dst[:, :], ang[:, src, :], ACT.Sin).then_inc(p_sin, 1)

            def split_hi(name, l, p, c=None):
                g = group_at(name, l, c)
                act.wait_ge(raw_in[p], 16 * (g + 1))
                if p < PAIRS - 1:
                    act.wait_ge(pair_used, g * (PAIRS - 1) + (p + 1))
                elif name == "qi":
                    act.wait_ge(full_s[7], uses_before(7, "gi0", l))
                elif name == "up0":
                    act.wait_ge(full_s[7], uses_before(7, "up13", l, c))
                else:
                    names = CHUNK if c is not None else PRE
                    prev = names[names.index(name) - 1]
                    b = bank_set(prev) + 3
                    act.wait_ge(full_s[b], uses_before(b, f"{prev}3", l, c) + 1)
                for src, hi, _ in pair_views(name, p):
                    last = af(hi, src, ACT.Copy)
                last.then_inc(hi_split, 1)

            def a_tile(l, blk, kk):
                n = l * 2 * DK + (blk * DK + kk)
                g, b = gains[:, 4 * blk, kk:kk + 1], gains[:, 4 * blk + 1, kk:kk + 1]
                act.wait_ge(xn_ready, n + 1)
                act.wait_ge(a_lo_s, n + 1)
                af(full[:, kk % 2, :], x[:, kk, :], ACT.Identity, bias=b, scale=g)
                af(a_hi[:, kk, :], x[:, kk, :], ACT.Identity, bias=b, scale=g).then_inc(a_hi_s, 1)

            def scale_residual(blk):
                for kk in range(DK):
                    af(x[:, kk, :], x[:, kk, :], ACT.Identity, bias=gains[:, 4 * blk + 3, kk:kk + 1],
                       scale=gains[:, 4 * blk + 2, kk:kk + 1]).then_inc(x_scaled, 1)

            def slot(l, nxt, takeout, c=None, nc_=None):
                for p in range(PAIRS - 1):
                    split_hi(nxt, l, p, c if nc_ is None else nc_)
                takeout()
                split_hi(nxt, l, PAIRS - 1, c if nc_ is None else nc_)

            def ln_squares(l, base, ms, name, c=None):
                for m in ms:
                    b = bank_set(name) + m % 4
                    act.wait_ge(free_s[b], uses_before(b, f"{name}{m % 4}", l, c) + 1)
                    if m:
                        act.wait_ge(ln_q_s, base * (DK - 1) + m)
                    af(ln_sq[:, m % 2, :] if m else ln_q[:, :], x[:, m, :], ACT.Square).then_inc(ln_sq_s, 1)

            def ln_root(l, mean_name, n):
                b = uses_before(4, mean_name, l)
                act.wait_ge(full_s[4], b + 1)
                af(mean[:, :], banks[4][:, :], ACT.Copy)
                af(var[:, :], banks[4][:, :], ACT.Square).then_inc(free_s[4], 1)
                act.wait_ge(ln_var, n)
                af(var[:, :], var[:, :], ACT.Sqrt).then_inc(ln_std, 1)

            def layer(l):
                split_hi("qi", l, 0)
                split_hi("qi", l, 1)
                act.wait_ge(gains_ready, l * 2 + 1)
                for kk in range(DK):
                    a_tile(l, 0, kk)
                    if kk == 1:
                        split_hi("qi", l, 2)
                    if kk == 3:
                        split_hi("qi", l, 3)
                act.wait_ge(kiwi_in, 16 * (l + 1))
                af(kiwi_hi[:, :, :], kiwi_raw[:, :, :], ACT.Copy).then_inc(kiwi_hi_s, 1)
                scale_residual(0)

                def ring_free(t):
                    t -= 2
                    if 5 <= t < 9:
                        act.wait_ge(full_s[4], uses_before(4, f"vt{t - 5}", l) + 1)
                    elif t >= 0:
                        act.wait_ge(rope_done, l * 13 + (t + 1 if t < 5 else t - 3))

                def rope_tile(name, t, m):
                    b = m
                    ring_free(t)
                    act.wait_ge(full_s[b], uses_before(b, f"{name}{m}", l) + 1)
                    af(rraw[:, t % 2, :], banks[b][:, :], ACT.Copy)
                    af(rrot[0:64, t % 2, :], banks[b][64:P, :], ACT.Copy)
                    af(rrot[64:P, t % 2, :], banks[b][0:64, :], ACT.Copy).then_inc(free_s[b], 1)

                def qi_out():
                    for m in range(4):
                        rope_tile("qi", m, m)
                act.wait_ge(vec_ready, l + 1)
                slot(l, "xr", qi_out)
                ring_free(4)
                act.wait_ge(full_s[4], uses_before(4, "kiwi", l) + 1)
                af(rraw[0:KIWI, 0, :], banks[4][0:KIWI, :], ACT.Copy)
                af(rrot[0:32, 0, :], banks[4][32:64, :], ACT.Copy)
                af(rrot[32:64, 0, :], banks[4][0:32, :], ACT.Copy).then_inc(free_s[4], 1)

                def xr_out():
                    for m in range(LT):
                        act.wait_ge(full_s[m], uses_before(m, f"xr{m}", l) + 1)
                        af(xr[:, m, CONV - 1:], banks[m][:, :], ACT.Copy).then_inc(free_s[m], 1)
                slot(l, "yg", xr_out)
                act.wait_ge(full_s[4], uses_before(4, "wi", l) + 1)
                af(wi[:, :, :].rearrange("p t h -> p (t h)"), banks[4][:, 0:TT * IDX_HEADS], ACT.Copy,
                   scale=IDX_HEADS ** -0.5).then_inc(free_s[4], 1)

                def idx_relu(i):
                    if i == 1:
                        act.wait_ge(a_lo_s, l * 2 * DK + (DK + 2))
                    for h in range(IDX_HEADS):
                        u = IDX.index((i, h))
                        b = 5 + u % 2
                        act.wait_ge(full_s[b], uses_before(b, f"idx{u}", l) + 1)
                        act.wait_ge(idx_acc, l * len(IDX) + (u + 1))
                        af(rel[:, u % 2, 0:(i + 1) * P], banks[b][:, 0:(i + 1) * P], ACT.Relu).then_inc(free_s[b], 1)
                idx_relu(1)

                def yg_out():
                    for m in range(LT):
                        act.wait_ge(full_s[m], uses_before(m, f"yg{m}", l) + 1)
                        af(yg[:, m, :], banks[m][:, :], ACT.Gelu_apprx_tanh).then_inc(free_s[m], 1)
                slot(l, "v", yg_out)
                idx_relu(2)
                for m in range(LT):
                    for b, name, dst, bias in ((4, "gr", th, "b_gate_a"), (7, "gi", gi, "b_gate_x")):
                        act.wait_ge(full_s[b], uses_before(b, f"{name}{m}", l) + 1)
                        af(dst[:, m, :], banks[b][:, :], ACT.Sigmoid, bias=vcol(bias, m)).then_inc(free_s[b], 1)

                def v_out():
                    for m in range(HEADS):
                        ring_free(5 + m)
                        act.wait_ge(full_s[m], uses_before(m, f"v{m}", l) + 1)
                        af(rraw[:, (5 + m) % 2, :], banks[m][:, :], ACT.Copy).then_inc(free_s[m], 1)
                        vt_out(m - 1)

                def vt_out(m):
                    if m < 0:
                        return
                    act.wait_ge(full_s[4], uses_before(4, f"vt{m}", l) + 1)
                    af(v[:, :, m * DH:(m + 1) * DH], banks[4][:, :].rearrange("p (t d) -> p t d", t=TT),
                       ACT.Copy).then_inc(free_s[4], 1)
                for p in range(PAIRS - 1):
                    split_hi("k", l, p)
                act.wait_ge(conv_done, l * LT + LT)
                for m in range(LT):
                    act.wait_ge(free_s[4], uses_before(4, f"gr{m}", l) + 1)
                    af(lru_a[:, m, :], th[:, m, :], ACT.Exp, scale=neg_sp[:, m:m + 1])
                    af(th[:, m, :], th[:, m, :], ACT.Tanh, scale=vcol("lru_lambda", m)).then_inc(lru_exp, 1)
                split_hi("k", l, PAIRS - 1)
                idx_relu(3)
                v_out()
                vt_out(HEADS - 1)

                def k_out():
                    for m in range(HEADS):
                        rope_tile("k", 9 + m, m)
                split_hi("q", l, 0)
                split_hi("q", l, 1)
                for m in range(LT):
                    act.wait_ge(lru_m, l * LT + (m + 1))
                    af(th[:, m, :], th[:, m, :], ACT.Sqrt).then_inc(lru_sqrt, 1)
                split_hi("q", l, 2)
                k_out()
                split_hi("q", l, 3)

                def q_out():
                    act.wait_ge(lru_out, l * LT + LT)
                    for m in range(HEADS):
                        rope_tile("q", 13 + m, m)
                slot(l, "out0", q_out)
                for m in range(LT):
                    af(sq_l[:, m, :], xc[:, m, :], ACT.Square).then_inc(sq_ready, 1)

                def expo(u):
                    i, h = UNITS[u]
                    act.wait_ge(attn_max, l * 16 + (u + 1))
                    pr = probs[:, u % 2, 0:(i + 1) * P]
                    af(pr, pr, ACT.Exp, bias=negm[:, u:u + 1], scale=SCALE, accum_out=rsum[:, u:u + 1]).then_inc(attn_exp, 1)

                def probs_turned(u):
                    i, h = UNITS[u]
                    b = 2 + u % 2
                    act.wait_ge(full_s[b], uses_before(b, f"pt{u}", l) + 1)
                    if u >= 2:
                        i2, h2 = UNITS[u - 2]
                        if h2 == HEADS - 1:
                            act.wait_ge(full_s[i2 % 2], uses_before(i2 % 2, f"o{i2}", l) + 1)
                        else:
                            act.wait_ge(pv_done, l * 12 + (3 * i2 + h2 + 1))
                    n = (i + 1) * P
                    af(probs_t[:, u % 2, 0:n], banks[b][:, 0:n], ACT.Copy).then_inc(free_s[b], 1)

                def attn_tile_out(i):
                    b = i % 2
                    act.wait_ge(full_s[b], uses_before(b, f"o{i}", l) + 1)
                    af(ao[:, :, i * P:(i + 1) * P], banks[b][:, :].rearrange("p (h q) -> p h q", h=HEADS), ACT.Copy)
                    af(sq_a[:, i, :], banks[b][:, :], ACT.Square).then_inc(free_s[b], 1)

                for u in range(len(UNITS)):
                    expo(u)
                    if u >= 1:
                        probs_turned(u - 1)
                    if u >= 6 and (u - 2) % HEADS == 0:
                        attn_tile_out((u - 2) // HEADS - 1)
                probs_turned(len(UNITS) - 1)
                attn_tile_out(TT - 1)
                for b, name, dst, width in ((6, "lms", lru_rstd, LW), (5, "ams", attn_rstd, AW)):
                    act.wait_ge(full_s[b], uses_before(b, name, l) + 1)
                    af(dst[:, :], banks[b][:, :], ACT.Sqrt, scale=D / width, bias=eps[:, :]).then_inc(free_s[b], 1)
                for n, kk in enumerate(OUT_ORDER):
                    act.wait_ge(m_full, l * DK + (n + 2))
                    af(b_hi[:, kk, :], full[:, n % 2, :], ACT.Copy).then_inc(b_hi_s, 1)

                def out_out(j):
                    def run():
                        ln_squares(l, l * 2, range(4 * j, 4 * j + 4), f"out{j}")
                    return run
                slot(l, "out1", out_out(0))
                slot(l, "up0", out_out(1), nc_=0)
                ln_root(l, "mean", l * 2 + 1)
                act.wait_ge(gains_ready, l * 2 + 2)
                for kk in range(DK):
                    a_tile(l, 1, kk)
                scale_residual(1)

                def chunk(l, c, last):
                    def hidden(j):
                        def hi(t):
                            act.wait_ge(ff_sq, l * (NC * DK) + c * DK + (2 + t + 1))
                            if t == 0:
                                act.wait_ge(full_s[7], uses_before(7, "up13", l, c))
                            af(b_hi[:, t, :], ffsq[:, t % 2, :], ACT.Copy).then_inc(b_hi_s, 1)

                        def run():
                            for m in range(4):
                                t = 4 * j + m
                                b = bank_set(f"up{j}") + m
                                act.wait_ge(full_s[b], uses_before(b, f"up{j}{m}", l, c) + 1)
                                act.wait_ge(ff_sq, l * (NC * DK) + c * DK + (t + 1))
                                af(relu[:, t % 2, :], banks[b][:, :], ACT.Relu).then_inc(free_s[b], 1)
                                if m:
                                    hi(t - 1)
                            hi(4 * j + 3)
                        return run
                    slot(l, "up1", hidden(0), c)
                    slot(l, "down0", hidden(1), c)
                    if not last:
                        slot(l, "down1", lambda: None, c)
                        slot(l, "up0", lambda: None, c + 1)
                    else:
                        base = l * 2 + 1
                        slot(l, "down1", lambda: ln_squares(l, base, range(4), "down0", c), c)
                        ln_squares(l, base, range(4, 8), "down1", c)
                chunks(act, l, chunk)
                ln_root(l, "mean_b", l * 2 + 2)
            layers(act, layer)

            for m in range(DK):
                act.wait_ge(xn_ready, DEPTH * 2 * DK + (m + 1))
                af(x[:, m, :], x[:, m, :], ACT.Identity, bias=vcol("ln2_b", m), scale=vcol("ln2_g", m)).then_inc(y_ready, 1)
            for n in range(TT):
                for half in range(2):
                    b = 2 * (n % 2) + half
                    act.wait_ge(y_t, 2 * n + half + 1)
                    af(xs[:, n, half * T:(half + 1) * T], banks[b][:, :], ACT.Copy).then_inc(y_out, 1)

        @block.vector
        def _(ve):
            v_ = nc.vector
            step = Chain(ve, dve_step)
            tt, ts, stt = v_.tensor_tensor, v_.tensor_scalar, v_.scalar_tensor_tensor

            for s in full_s + free_s + [m_full, kiwi_lo_s]:
                ve.sem_inc(s, 1)
            ve.sem_inc(lo_split, PAIRS)
            ve.sem_inc(pair_used, PAIRS - 1)
            ve.sem_inc(mod_used, 2)
            ve.sem_inc(a_lo_s, 2)
            ve.sem_inc(ff_sq, 2)
            ve.sem_inc(idx_acc, 2)
            ve.sem_inc(ln_q_s, 2)
            step(v_.memset(mean[:, :], 0.0))
            step(v_.memset(rstd[:, :], 1.0))
            step(v_.memset(gains[:, 4:6, :], 1.0))
            ve.wait_ge(p_sin, 1)
            tt(csil[:, :], csil[:, :], vecs[:, 0, NV:P], ALU.mult).then_inc(p_dve, 1)
            ve.wait_ge(p_sin, 3)
            e, z, z2, s_ = (spt[:, n, :, :] for n in range(4))
            at, n = VEC["lru_lambda"]
            lam = vecs[:, :, at:at + n]
            step(ts(z, e, 2.0, None, ALU.add))
            step.settle()
            step(v_.reciprocal(z, z))
            step.settle()
            step(tt(z, z, e, ALU.mult))
            step.settle()
            step(tt(z2, z, z, ALU.mult))
            step.settle()
            step(ts(s_, z2, 1.0 / 17, None, ALU.mult))
            for odd in range(15, 1, -2):
                step.settle()
                step(stt(s_, s_, 1.0 / odd, z2, ALU.add, ALU.mult))
            step.settle()
            step(stt(s_, s_, 1.0, z, ALU.add, ALU.mult))
            step(ts(lam, lam, -1.0, 0.0, ALU.mult, ALU.max))
            step.settle()
            step(stt(lam, s_, 2.0, lam, ALU.mult, ALU.add))
            step.settle()
            step(ts(lam, lam, LRU_C, None, ALU.mult))
            ve.wait_ge(p_in_pos, 32)
            step(v_.tensor_copy(posf[:, :], pos[:, :]))
            step.settle()
            for n in range(2):
                step(ts(ang[:, n, :], posf[:, :], freq[:, n:n + 1], None, ALU.mult))
            step.settle()
            for n in range(2):
                step(ts(ang[:, 2 + n, :], ang[:, n, :], 1.0 / (2 * np.pi), ROUND, ALU.mult, ALU.add))
            step.settle()
            for n in range(2):
                step(ts(ang[:, 2 + n, :], ang[:, 2 + n, :], -ROUND, None, ALU.add))
            for part in TWO_PI:
                step.settle()
                for n in range(2):
                    step(stt(ang[:, n, :], ang[:, 2 + n, :], -part, ang[:, n, :], ALU.mult, ALU.add))
            step.settle()
            for n in range(2):
                step(ts(ang[:, n, :], ang[:, n, :], PI_IN, -PI_IN, ALU.min, ALU.max))
            step.settle()
            for n in range(2):
                step(stt(ang[:, 2 + n, :], ang[:, n, :], -1.0, ang[:, n, :], ALU.mult, ALU.min))
            step.settle()
            for n in range(2):
                step(ts(ang[:, 2 + n, :], ang[:, 2 + n, :], float(np.pi / 2), None, ALU.add))
            step.settle()
            ve.sem_inc(p_ang, 1)

            def next_gains(l_next, g_prev, b_prev):
                at, _ = VEC["b_mod"]
                step(tt(modn[:, :].rearrange("p (one n) -> p one n", one=1),
                        modn[:, :].rearrange("p (one n) -> p one n", one=1),
                        vecs[:, bass.ds(l_next, 1), at:at + MODS_NEXT], ALU.add))
                step.settle()
                fold_gains(0, modn[:, 0:DK], modn[:, DK:2 * DK], g_prev, b_prev)

            def fold_gains(blk, shift, scale, g, b):
                G, B, RG, RB = (gains[:, 4 * blk + n, :] for n in range(4))
                step(ts(RG, g, ALPHA, None, ALU.mult))
                step(ts(RB, b, ALPHA, None, ALU.mult))
                step(stt(G, scale, 1.0, g, ALU.add, ALU.mult))
                step(stt(B, scale, 1.0, b, ALU.add, ALU.mult))
                step.settle()
                tt(B, B, shift, ALU.add).then_inc(gains_ready, 1)

            ve.wait_ge(mod_used, 2 + MODS_NEXT)
            v_.tensor_copy(modn[:, :], banks[7][:, 0:MODS_NEXT]).then_inc(p_dve, 1)
            ve.wait_ge(p_dve, 2)
            step(v_.memset(gains[:, 5, :], 0.0))
            step.settle()
            next_gains(0, gains[:, 4, :], gains[:, 5, :])
            ve.wait_ge(p_act, 1 + DK)
            ve.wait_ge(p_const, 9)
            step.restart()

            def split_lo(name, l, p, c=None):
                g = group_at(name, l, c)
                ve.wait_ge(hi_split, g * PAIRS + (p + 1))
                for src, hi, lo in pair_views(name, p):
                    last = tt(lo, src, hi.bitcast(F32), ALU.subtract)
                last.then_inc(lo_split, 1)

            def norm_tile(kk):
                xk = x[:, kk, :]
                step(tt(xk, xk, mean[:, :], ALU.subtract))
                step.settle()
                tt(xk, xk, rstd[:, :], ALU.mult).then_inc(xn_ready, 1)

            def a_lo_tile(l, blk, kk):
                ve.wait_ge(a_hi_s, l * 2 * DK + (blk * DK + kk + 1))
                tt(a_lo[:, kk, :], full[:, kk % 2, :], a_hi[:, kk, :].bitcast(F32), ALU.subtract).then_inc(a_lo_s, 1)

            def ln_stats(l, mean_name, e2_name, n):
                ve.wait_ge(free_s[4], uses_before(4, mean_name, l) + 1)
                ve.wait_ge(full_s[5], uses_before(5, e2_name, l) + 1)
                stt(var[:, :], var[:, :], -1.0, banks[5][:, :], ALU.mult, ALU.add).then_inc(free_s[5], 1)
                ve.wait_ge(free_s[5], uses_before(5, e2_name, l) + 1)
                ts(var[:, :], var[:, :], 0.0, LN_EPS, ALU.max, ALU.add).then_inc(ln_var, 1)
                ve.wait_ge(ln_std, n)
                step(v_.reciprocal(rstd[:, :], var[:, :]))
                step.settle()

            def residual(l, name, m, gate, c=None):
                b = bank_set(name) + m % 4
                ve.wait_ge(full_s[b], uses_before(b, f"{name}{m % 4}", l, c) + 1)
                stt(x[:, m, :], banks[b][:, :], mods[:, gate * DK + m:gate * DK + m + 1], x[:, m, :],
                    ALU.mult, ALU.add).then_inc(free_s[b], 1)

            def ln_sum(l, name, m, c=None):
                b = bank_set(name) + m % 4
                ve.wait_ge(free_s[b], uses_before(b, f"{name}{m % 4}", l, c) + 1)
                if m == 0:
                    step(v_.tensor_copy(ln_s[:, :], x[:, 0, :]))
                else:
                    step.settle()
                    ins = tt(ln_s[:, :], ln_s[:, :], x[:, m, :], ALU.add)
                    if m == DK - 1:
                        ins.then_inc(ln_s_s, 1)
                    else:
                        step(ins)

            def slot(l, nxt, work, c=None, nc_=None):
                cn = c if nc_ is None else nc_
                for p in range(PAIRS - 1):
                    split_lo(nxt, l, p, cn)
                    work[p]()
                split_lo(nxt, l, PAIRS - 1, cn)

            def none():
                pass

            def layer(l):
                norm_tile(0)
                split_lo("qi", l, 0)
                for kk in range(1, DK):
                    norm_tile(kk)
                    a_lo_tile(l, 0, kk - 1)
                    if kk in (2, 4, 5):
                        split_lo("qi", l, (2, 4, 5).index(kk) + 1)
                a_lo_tile(l, 0, DK - 1)
                step(v_.memset(xr[:, :, 0:CONV - 1], 0.0))
                step(v_.tensor_copy(vec[:, :].rearrange("p (one n) -> p one n", one=1), vecs[:, bass.ds(l, 1), 0:NV]))
                ve.wait_ge(kiwi_hi_s, l + 1)
                tt(kiwi_lo[:, :, :], kiwi_raw[:, :, :], kiwi_hi[:, :, :].bitcast(F32), ALU.subtract).then_inc(kiwi_lo_s, 1)
                step.settle()
                step(ts(neg_sp[:, :], vcol("lru_lambda", 0, LT), -1.0, None, ALU.mult))
                step.settle()
                ve.sem_inc(vec_ready, 1)

                def rope(name, t, m, dst, cos, sin):
                    s = t % 2
                    ve.wait_ge(free_s[m], uses_before(m, f"{name}{m}", l) + 1)
                    step(tt(rraw[:, s, :], rraw[:, s, :], cos[:, :], ALU.mult))
                    step(tt(rrot[:, s, :], rrot[:, s, :], sin[:, :], ALU.mult))
                    step.settle()
                    tt(dst, rraw[:, s, :], rrot[:, s, :], ALU.add).then_inc(rope_done, 1)

                def qi_out():
                    for m in range(4):
                        rope("qi", m, m, qi[:, m, :], cos_i, sin_i)
                slot(l, "xr", (none, none, qi_out))
                ve.wait_ge(free_s[4], uses_before(4, "kiwi", l) + 1)
                step(tt(rraw[0:64, 0, :], rraw[0:64, 0, :], cos_i[0:64, :], ALU.mult))
                step(tt(rrot[0:64, 0, :], rrot[0:64, 0, :], sin_i[0:64, :], ALU.mult))
                step.settle()
                tt(ki_a[0:32, :], rraw[0:32, 0, :], rrot[0:32, 0, :], ALU.add)
                tt(ki_b[32:64, :], rraw[0:32, 0, :], rrot[0:32, 0, :], ALU.add)
                tt(ki_a[64:96, :], rraw[32:64, 0, :], rrot[32:64, 0, :], ALU.subtract)
                tt(ki_b[96:P, :], rraw[32:64, 0, :], rrot[32:64, 0, :], ALU.subtract).then_inc(rope_done, 1)

                def idx_add(i):
                    if i == 1:
                        ve.wait_ge(free_s[4], uses_before(4, "wi", l) + 1)
                    for h in range(IDX_HEADS):
                        u = IDX.index((i, h))
                        b = 5 + u % 2
                        n = (i + 1) * P
                        ve.wait_ge(free_s[b], uses_before(b, f"idx{u}", l) + 1)
                        if h:
                            ve.wait_ge(idx_acc, l * len(IDX) + (2 + u))
                        stt(acc_of(i), rel[:, u % 2, 0:n], wi[:, i, h:h + 1],
                            acc_of(i) if h else causal[:, (TT - 1 - i) * P:TT * P], ALU.mult, ALU.add).then_inc(idx_acc, 1)

                rounds = [0]
                per = TOPK // 8

                def topk(upto):
                    for r in range(rounds[0], upto):
                        i = 1 + r // per
                        if r % per == 0:
                            ve.wait_ge(idx_acc, l * len(IDX) + (2 + i * IDX_HEADS))
                            ve.sem_inc(dve_step, 1)
                            step.n += 1
                        step.settle()
                        step(v_.max(best[:, :], acc_of(i)))
                        step.settle()
                        step(v_.match_replace(acc_of(i), best[:, :], acc_of(i), TAKEN))
                        if r % per == per - 1:
                            step.settle()
                            step(ts(acc_of(i), acc_of(i), TAKEN, -BIG, ALU.not_equal, ALU.mult))
                    rounds[0] = max(rounds[0], upto)

                def conv(m):
                    if m == 0:
                        step.settle()
                    ve.wait_ge(free_s[m], uses_before(m, f"xr{m}", l) + 1)
                    for j in range(CONV):
                        w = vcol("conv_w", j * LT + m)
                        src = xr[:, m, j:j + T]
                        if j == 0:
                            step(ts(xc[:, m, :], src, w, vcol("conv_b", m), ALU.mult, ALU.add))
                        else:
                            step.settle()
                            ins = stt(xc[:, m, :], src, w, xc[:, m, :], ALU.mult, ALU.add)
                            if j == CONV - 1:
                                ins.then_inc(conv_done, 1)
                            else:
                                step(ins)

                slot(l, "yg", (none, none, none))
                idx_add(1)
                slot(l, "v", (lambda: conv(0), lambda: (conv(1), conv(2)), lambda: conv(3)))
                idx_add(2)

                def lru_input(m):
                    ve.wait_ge(free_s[7], uses_before(7, f"gi{m}", l) + 1)
                    ve.wait_ge(conv_done, l * LT + (m + 1))
                    step(tt(xc[:, m, :], xc[:, m, :], gi[:, m, :], ALU.mult))
                    ve.wait_ge(lru_exp, l * LT + (m + 1))
                    step.settle()
                    step(tt(gi[:, m, :], lru_a[:, m, :], lru_a[:, m, :], ALU.mult))
                    step.settle()
                    stt(th[:, m, :], gi[:, m, :], 1.0, th[:, m, :], ALU.add, ALU.mult).then_inc(lru_m, 1)

                def lru_scan(m):
                    ve.wait_ge(lru_sqrt, l * LT + (m + 1))
                    step(tt(th[:, m, :], th[:, m, :], xc[:, m, :], ALU.mult))
                    step.settle()
                    step(v_.tensor_tensor_scan(gi[:, m, :], lru_a[:, m, :], th[:, m, :], 0.0, ALU.mult, ALU.add))
                    step.settle()
                    tt(xc[:, m, :], gi[:, m, :], yg[:, m, :], ALU.mult).then_inc(lru_out, 1)

                slot(l, "k", (lambda: topk(4), lambda: topk(8), lambda: topk(12)))
                idx_add(3)
                for m in range(LT):
                    lru_input(m)

                def scans():
                    for m in range(LT):
                        lru_scan(m)

                def k_out():
                    for m in range(HEADS):
                        rope("k", 9 + m, m, k[:, m, :], cos_m, sin_m)
                slot(l, "q", (lambda: topk(16), scans, k_out))

                def q_out():
                    topk(24)
                    for m in range(HEADS):
                        rope("q", 13 + m, m, q[:, m, :], cos_m, sin_m)
                slot(l, "out0", (lambda: topk(20), lambda: topk(22), q_out))

                def mask_scores(u):
                    i, h = UNITS[u]
                    b = 5 + u % 2
                    n = (i + 1) * P
                    ve.wait_ge(full_s[b], uses_before(b, f"s{u}", l) + 1)
                    if u >= 2:
                        ve.wait_ge(full_s[2 + u % 2], uses_before(2 + u % 2, f"pt{u - 2}", l) + 1)
                    pr = probs[:, u % 2, 0:n]
                    tt(pr, banks[b][:, 0:n], bias_of(i), ALU.add).then_inc(free_s[b], 1)
                    ve.wait_ge(free_s[b], uses_before(b, f"s{u}", l) + 1)
                    step(v_.reduce_max(mx[:, u:u + 1], pr, AX_X))
                    step.settle()
                    ts(negm[:, u:u + 1], mx[:, u:u + 1], -SCALE, None, ALU.mult).then_inc(attn_max, 1)

                def normalize(u):
                    i, h = UNITS[u]
                    ve.wait_ge(attn_exp, l * 16 + (u + 1))
                    step(v_.reciprocal(rinv[:, u:u + 1], rsum[:, u:u + 1]))
                    step.settle()
                    pr = probs[:, u % 2, 0:(i + 1) * P]
                    ts(pr, pr, rinv[:, u:u + 1], None, ALU.mult).then_inc(attn_p, 1)

                for u in range(len(UNITS)):
                    i, h = UNITS[u]
                    if i:
                        topk(i * per)
                        step.settle()
                    mask_scores(u)
                    topk(min(24 + 4 * (u + 1), 3 * per))
                    if u:
                        normalize(u - 1)
                normalize(len(UNITS) - 1)

                at, _ = VEC["b_mod"]
                ve.wait_ge(mod_used, 2 + MODS_NEXT + l * (6 * DK) + MODS_LATE)
                tt(mods[:, MODS_NEXT:], banks[7][:, 0:MODS_LATE], vec[:, at + MODS_NEXT:at + 6 * DK], ALU.add).then_inc(mods_out, 1)
                ve.wait_ge(mods_out, l * (NC + 1) + 1)
                for gate in (2, 5):
                    step(ts(mods[:, gate * DK:(gate + 1) * DK], mods[:, gate * DK:(gate + 1) * DK], 1.0, None, ALU.add))
                fold_gains(1, mods[:, 3 * DK:4 * DK], mods[:, 4 * DK:5 * DK], vcol("ln1_g", 0, DK), vcol("ln1_b", 0, DK))

                for b, name, dst in ((6, "lms", lru_rstd), (5, "ams", attn_rstd)):
                    ve.wait_ge(free_s[b], uses_before(b, name, l) + 1)
                    step(v_.reciprocal(dst[:, :], dst[:, :]))
                step.settle()

                def merged_lo(n):
                    kk = OUT_ORDER[n]
                    ve.wait_ge(b_hi_s, l * (5 * DK) + (n + 1))
                    tt(b_lo[:, kk, :], full[:, n % 2, :], b_hi[:, kk, :].bitcast(F32), ALU.subtract).then_inc(b_lo_s, 1)
                for n, kk in enumerate(OUT_ORDER):
                    if kk >= HEADS:
                        src, g, r = xc[:, kk - HEADS, :], vcol("g_lru_out", kk - HEADS), lru_rstd
                    else:
                        src, g, r = ao[:, kk, :], vcol("g_attn_out", kk), attn_rstd
                    if n >= 2:
                        ve.wait_ge(b_lo_s, l * (5 * DK) + (n - 1))
                    stt(full[:, n % 2, :], src, g, r[:, :], ALU.mult, ALU.mult).then_inc(m_full, 1)
                    if n:
                        merged_lo(n - 1)
                merged_lo(DK - 1)

                ve.wait_ge(x_scaled, l * 2 * DK + DK)

                def out_out(j):
                    def run():
                        for m in range(4 * j, 4 * j + 4):
                            residual(l, f"out{j}", m, 2)
                            ln_sum(l, f"out{j}", m)
                    return run
                slot(l, "out1", (none, none, out_out(0)))
                slot(l, "up0", (none, none, out_out(1)), nc_=0)
                ln_stats(l, "mean", "e2", l * 2 + 1)
                norm_tile(0)
                for kk in range(1, DK):
                    norm_tile(kk)
                    a_lo_tile(l, 1, kk - 1)
                a_lo_tile(l, 1, DK - 1)
                step.restart()

                def chunk(l, c, last):
                    def hidden(j):
                        b0 = l * (5 * DK) + c * DK + DK

                        def lo(t):
                            ve.wait_ge(b_hi_s, b0 + (t + 1))
                            tt(b_lo[:, t, :], ffsq[:, t % 2, :], b_hi[:, t, :].bitcast(F32), ALU.subtract).then_inc(b_lo_s, 1)

                        def run():
                            for m in range(4):
                                t = 4 * j + m
                                b = bank_set(f"up{j}") + m
                                ve.wait_ge(free_s[b], uses_before(b, f"up{j}{m}", l, c) + 1)
                                ve.wait_ge(b_hi_s, b0 + t - 1)
                                ve.wait_ge(b_lo_s, b0 + t - 1)
                                tt(ffsq[:, t % 2, :], relu[:, t % 2, :], relu[:, t % 2, :], ALU.mult).then_inc(ff_sq, 1)
                                if m:
                                    lo(t - 1)
                            lo(4 * j + 3)
                        return run

                    def mods_next():
                        ve.wait_ge(mod_used, (2 + MODS_NEXT + l * (6 * DK) + MODS_LATE) + c * 4 + 4)
                        v_.tensor_copy(modn[:, bass.ds(c * 4, 4)], banks[4][:, 0:4]).then_inc(mods_out, 1)

                    def down_out(j):
                        def run():
                            if j == 0:
                                mods_next()
                            for m in range(4 * j, 4 * j + 4):
                                residual(l, f"down{j}", m, 5, c)
                                if last:
                                    ln_sum(l, f"down{j}", m, c)
                        return run
                    slot(l, "up1", (none, none, hidden(0)), c)
                    if not last:
                        slot(l, "down0", (none, none, hidden(1)), c)
                        ve.wait_ge(x_scaled, (l + 1) * 2 * DK)
                        slot(l, "down1", (none, none, down_out(0)), c)
                        slot(l, "up0", (none, none, down_out(1)), c + 1)
                    else:
                        slot(l, "down0", (none, none, hidden(1)), c)
                        slot(l, "down1", (none, none, down_out(0)), c)
                        ve.wait_ge(mods_out, (l + 1) * (NC + 1))
                        next_gains((l + 1) % DEPTH, vcol("ln2_g", 0, DK), vcol("ln2_b", 0, DK))
                        down_out(1)()
                    step.restart()
                chunks(ve, l, chunk)
                ln_stats(l, "mean_b", "e2_b", l * 2 + 2)
                step.restart()
            layers(ve, layer)
            for kk in range(DK):
                norm_tile(kk)


ROUND = 1.5 * 2.0 ** 23
TWO_PI = (6.28125, 0.001934051513671875, 2 * np.pi - 6.28125 - 0.001934051513671875)
PI_IN = 3.1415925

INS = ["x", "c", "positions", "w_mod", "b_mod", "w_in", "conv_w", "conv_b", "w_gate_a", "b_gate_a", "w_gate_x",
       "b_gate_x", "lru_lambda", "g_attn_out", "g_lru_out", "w_out", "ln1_g", "ln1_b", "w_up", "w_down", "ln2_g", "ln2_b"]


def rope_frequencies():
    out = np.zeros((P, 2), np.float32)
    for col, (dim, per) in enumerate(((DH, 64), (IDX_DH, 32))):
        inv = np.float32(THETA) ** (-np.arange(0, dim, 2, dtype=np.float32) / np.float32(dim))
        p = np.arange(P)
        out[:, col] = inv[p % per] * np.where(p < 64, -1, 1)
    return out


def kernel(**inputs):
    import concourse.bacc as bacc
    from concourse.bass_utils import run_bass_kernel_spmd

    nc = bacc.Bacc("TRN2", target_bir_lowering=False, num_devices=1)
    arrays, args = {}, {}
    for name, a in [(n, inputs[n]) for n in INS] + [("freq", rope_frequencies())]:
        a = np.ascontiguousarray(a)
        arrays[f"in_{name}_dram"] = a
        args[name] = nc.dram_tensor(f"in_{name}_dram", a.shape, mybir.dt.from_np(a.dtype), kind="ExternalInput").ap()
    out = nc.dram_tensor("out_dram", (1, T, D), F32, kind="ExternalOutput").ap()
    trunk_kernel(nc, args, out)
    r = run_bass_kernel_spmd(nc, [arrays], core_ids=[0])
    return r.results[0]["out_dram"]
```

```python
import numpy as np

import concourse.bass as bass
from concourse import mybir
from contextlib import ExitStack

F32 = mybir.dt.float32
F32R = mybir.dt.float32r
I32 = mybir.dt.int32
ALU = mybir.AluOpType
ACT = mybir.ActivationFunctionType
AX_X = mybir.AxisListType.X

P = 128
DEPTH, D, T, DFF = 2, 1024, 512, 4096
DK = D // P
TT = T // P
HEADS, DH = 4, 128
IDX_HEADS, IDX_DH = 8, 64
TOPK = min(256, T // 4)
AW = HEADS * DH
LW = D - AW
LT = LW // P
CONV = 4
LRU_C = 8.0
LN_EPS = 1e-5
ALPHA = (2.0 * DEPTH) ** 0.25
THETA = 10000.0
SCALE = DH ** -0.5
BIG = 3.0e38
TAKEN = -3.4e38

COL = {}
_at = 0
for _name, _n in (("q", AW), ("k", AW), ("v", AW), ("qi", IDX_HEADS * IDX_DH), ("kiwi", IDX_DH + IDX_HEADS),
                  ("xr", LW), ("yg", LW)):
    COL[_name] = _at
    _at += _n
KIWI = IDX_DH + IDX_HEADS

PRE = ["qi", "xr", "yg", "v", "k", "q", "out0", "out1"]
CHUNK = ["up0", "up1", "down0", "down1"]
NC = DFF // D
PAIRS = 4
GROUPS = len(PRE) + NC * len(CHUNK)
OUT_ORDER = [4, 5, 6, 7, 0, 1, 2, 3]

MR = 2

VEC = {}
_at = 0
for _name, _n in (("b_mod", 6 * DK), ("conv_w", CONV * LT), ("conv_b", LT), ("b_gate_a", LT), ("b_gate_x", LT),
                  ("lru_lambda", LT), ("g_attn_out", HEADS), ("g_lru_out", LT), ("ln1_g", DK), ("ln1_b", DK),
                  ("ln2_g", DK), ("ln2_b", DK)):
    VEC[_name] = (_at, _n)
    _at += _n
NV = _at
MODS_NEXT = 2 * DK
MODS_LATE = 4 * DK
NEXT_PAIRS, LATE_PAIRS, MOD_PAIRS = DK, 2 * DK, 3 * DK
MOD_ROWS = LATE_PAIRS // 2

UNITS = [(i, h) for i in range(TT) for h in range(HEADS)]
IDX = [(i, h) for i in range(1, TT) for h in range(IDX_HEADS)]
_pre = {b: [n + str(b) for n in PRE[:6]] for b in range(4)}
for _b in (0, 1):
    _pre[_b] += [f"o{i}" for i in range(TT) if i % 2 == _b]
for _b in (2, 3):
    _pre[_b] += [f"pt{u}" for u in range(len(UNITS)) if u % 2 == _b - 2]
for _b in range(4):
    _pre[_b] += [f"out0{_b}"]
_pre[4] = (["kiwi", "wi"] + [f"vt{m}" for m in range(HEADS)] + [f"gr{m}" for m in range(LT)] +
           ["lms", "lrb", "out10", "sums", "rb"])
_pre[5] = ([f"idx{u}" for u in range(0, len(IDX), 2)] + [f"gi{m}" for m in range(0, LT)] +
           [f"s{u}" for u in range(0, 16, 2)] + ["ams", "arb", "out11", "mb"])
_pre[6] = [f"idx{u}" for u in range(1, len(IDX), 2)] + [f"s{u}" for u in range(1, 16, 2)] + ["out12"]
_pre[7] = ["out13"]
_chunk = {b: [f"up0{b}", f"down0{b}"] for b in range(4)}
for _b in range(4):
    _chunk[4 + _b] = [f"up1{_b}", f"down1{_b}"]
_post = {b: [] for b in range(8)}
_post[4], _post[5] = ["sums_b", "rb_b"], ["mb_b"]


def uses_before(b, name, l, c=None):
    per = len(_pre[b]) + NC * len(_chunk[b]) + len(_post[b])
    if c is not None:
        return l * per + c * len(_chunk[b]) + (len(_pre[b]) + _chunk[b].index(name) + 1)
    if name in _post[b]:
        return l * per + (len(_pre[b]) + NC * len(_chunk[b]) + _post[b].index(name) + 1)
    return l * per + (_pre[b].index(name) + 1)


def group_at(name, l, c=None):
    if c is None:
        return l * GROUPS + PRE.index(name)
    return l * GROUPS + c * len(CHUNK) + (len(PRE) + CHUNK.index(name))


def bank_set(name):
    return 4 if name in ("out1", "up1", "down1") else 0


ACC_AT = {1: 0, 2: 2 * P, 3: 5 * P}


def trunk_kernel(nc, A, out):
    ctx = ExitStack()
    with ctx:
        top = [(nc.sbuf_base + 63) // 64 * 64]

        def place(nbytes):
            at = top[0]
            top[0] += (nbytes + 31) // 32 * 32
            assert top[0] <= nc.sbuf_usable_end, (top[0], nc.sbuf_usable_end)
            return at

        def sb(name, shape, dt=F32, at=None):
            n = 4 * int(np.prod(shape[1:]))
            return nc.alloc_sbuf_tensor_at(name, shape, dt, offset=place(n) if at is None else at)

        K2 = 4 * T
        x = sb("resid", [P, DK, T])
        a_at = place(16 * K2)
        a_hi = sb("a_hi", [P, DK, T], F32R, a_at)
        a_lo = sb("a_lo", [P, DK, T], F32R, a_at + 8 * K2)
        th = sb("lru_root", [P, LT, T], F32, a_at)
        gi = sb("lru_gate", [P, LT, T], F32, a_at + 4 * K2)
        lru_a = sb("lru_a", [P, LT, T], F32, a_at + 8 * K2)
        sq_l = sb("lru_sq", [P, LT, T], F32, a_at + 12 * K2)
        mod_rows = sb("mod_rows", [MOD_ROWS, T], F32, a_at)
        b_at = place(16 * K2)
        b_hi = sb("b_hi", [P, DK, T], F32R, b_at)
        b_lo = sb("b_lo", [P, DK, T], F32R, b_at + 8 * K2)
        qi = sb("qi_rot", [P, 4, T], F32, b_at)
        ao = sb("attn_out", [P, HEADS, T], F32, b_at)
        q = sb("q_rot", [P, HEADS, T], F32, b_at + 4 * K2)
        k = sb("k_rot", [P, HEADS, T], F32, b_at + 8 * K2)
        v = sb("v_tok", [P, TT, AW], F32, b_at + 12 * K2)
        xs = sb("x_in", [P, TT, D], F32, b_at)
        raw = sb("w_raw", [P, PAIRS, 2, T])
        w_hi = sb("w_hi", [P, PAIRS, 2, T], F32R)
        w_lo_at = place(8 * K2)
        w_lo = sb("w_lo", [P, PAIRS, 2, T], F32R, w_lo_at)
        kiwi_raw = sb("kiwi_raw", [P, DK, KIWI], F32, b_at + 12 * K2)
        kiwi_hi = sb("kiwi_hi", [P, DK, KIWI], F32R, b_at + 12 * K2 + 4 * DK * KIWI)
        kiwi_lo = sb("kiwi_lo", [P, DK, KIWI], F32R, b_at + 12 * K2 + 8 * DK * KIWI)
        mod_at = place(MR * 8 * DK * P)
        mod_raw = sb("mod_raw", [P, MR, DK, 2 * P], F32, mod_at)
        first_mod = [sb(f"first_mod{n}", [P, DK, 2 * P], F32, at) for n, at in enumerate(
            [mod_at, mod_at + 4 * K2, a_at, a_at + 4 * K2, a_at + 8 * K2, a_at + 12 * K2, w_lo_at, w_lo_at + 4 * K2])]
        ki_a = sb("ki_even", [P, T])
        ki_b = sb("ki_odd", [P, T])
        xr_at = place(4 * LT * (T + CONV - 1))
        xr = sb("xr", [P, LT, T + CONV - 1], F32, xr_at)
        probs = sb("probs", [P, 4, T], F32, xr_at)
        ln_sq = sb("ln_sq", [P, 2, T], F32, xr_at)
        xc_at = place(4 * K2)
        xc = sb("xc", [P, LT, T], F32, xc_at)
        rstd = sb("ln_rstd", [P, T], F32, xc_at)
        mrstd = sb("ln_mrstd", [P, T], F32, xc_at + K2)
        yg_at = place(4 * K2)
        yg = sb("gelu_gate", [P, LT, T], F32, yg_at)
        ang = sb("angles", [P, 4, T], F32, yg_at)
        cos_m, sin_m, cos_i, sin_i = (sb(n, [P, T]) for n in ("cos_m", "sin_m", "cos_i", "sin_i"))
        acc_at = place(4 * 9 * P)
        acc = sb("idx_acc", [P, 9 * P], F32, acc_at)
        ln_s = sb("ln_s", [P, T], F32, acc_at)
        ln_q = sb("ln_q", [P, T], F32, acc_at + K2)
        causal = sb("causal", [P, TT * P])
        full_at = place(2 * K2)
        rel = sb("idx_rel", [P, 2, T], F32, full_at)
        probs_t = sb("probs_t", [P, 2, T], F32, full_at)
        full = sb("unsplit", [P, 2, T], F32, full_at)
        diag = sb("diag", [P, 2, TT, P], F32, full_at)
        diag_l = sb("diag_lru", [P, TT, P], F32, acc_at)
        diag_a = sb("diag_attn", [P, TT, P], F32, acc_at + K2)
        rope_at = place(4 * K2)
        rraw = sb("rope_raw", [P, 2, T], F32, rope_at)
        rrot = sb("rope_swapped", [P, 2, T], F32, rope_at + 2 * K2)
        relu = sb("ff_relu", [P, 2, T], F32, rope_at)
        ffsq = sb("ff_square", [P, 2, T], F32, rope_at + 2 * K2)
        sq_a = sb("attn_sq", [P, TT, T], F32, rope_at)
        pos = sb("positions_b", [P, T], I32, rope_at)
        turns_i = sb("turns_i", [P, T], I32, rope_at + K2)
        posf = sb("positions_f", [P, T], F32, rope_at + 2 * K2)
        stage = sb("vec_rows", [P, DEPTH, P], F32, full_at)
        blk = sb("gate_blocks", [P, 2, LT, P])
        vecs = sb("vecs", [P, DEPTH, P])
        vec = sb("vec", [P, NV])
        ident = sb("ident", [P, P])
        ident_d = sb("ident_d", [P, P])
        ones_d = sb("ones_d", [P, P])
        csil = sb("csil", [P, DK])
        csil_w = sb("csil_window", [P, DK, 2 * MOD_ROWS - 1])
        csil_d = sb("csil_d", [P, DK])
        mods = sb("mods", [P, 6 * DK])
        modn = sb("modn", [P, MODS_NEXT])
        gains = sb("gains", [P, 8, DK])
        small = sb("small", [P, 4, 16])
        wi = sb("wi", [P, TT, IDX_HEADS])
        best = sb("best", [P, 8])
        eps = sb("eps", [P, 1])
        stat = sb("stat", [P, 8, TT])
        neg_sp = sb("neg_sp", [P, LT])
        freq = sb("freq", [P, 2])
        spt = sb("spt", [P, 4, DEPTH, LT])
        mx, negm, rsum, rinv = (small[:, n, :] for n in range(4))

        banks = [ctx.enter_context(nc.psum_tensor(f"bank{b}", [P, T], F32)) for b in range(8)]

        def sem(name):
            return ctx.enter_context(nc.semaphore(name))

        full_s = [sem(f"bank_full{b}") for b in range(8)]
        free_s = [sem(f"bank_free{b}") for b in range(8)]
        raw_in = [sem(f"raw_in{s}") for s in range(PAIRS)]
        kiwi_in, kiwi_hi_s, kiwi_lo_s = sem("kiwi_in"), sem("kiwi_hi_done"), sem("kiwi_lo_done")
        hi_split, lo_split = sem("hi_split"), sem("lo_split")
        pair_used = sem("pair_used")
        mod_in = [sem(f"mod_in{s}") for s in range(MR)]
        first_mod_in = [sem(f"first_mod_in{n}") for n in range(NEXT_PAIRS)]
        mods_out = sem("mods_out")
        mod_used = sem("mod_used")
        mod_rows_s, mods_turned = sem("mod_rows_out"), sem("mods_turned")
        mod_sum = sem("mod_sum")
        gate_in = sem("gate_in")
        xn_ready = sem("xn_ready")
        a_hi_s, a_lo_s = sem("a_hi_done"), sem("a_lo_done")
        x_scaled = sem("x_scaled")
        m_full, b_hi_s, b_lo_s = sem("merged_full"), sem("b_hi_done"), sem("b_lo_done")
        ff_sq = sem("ff_squared")
        rope_done = sem("rope_done")
        idx_acc = sem("idx_accumulated")
        conv_done, lru_exp, lru_m, lru_sqrt, lru_out = (sem(n) for n in ("conv_done", "lru_exp", "lru_m", "lru_sqrt", "lru_out"))
        attn_max, attn_exp, attn_p = sem("attn_max"), sem("attn_exp"), sem("attn_p")
        pv_done = sem("pv_done")
        sq_ready = sem("squares_ready")
        ln_sq_s, ln_q_s, ln_s_s = sem("ln_squared"), sem("ln_q_added"), sem("ln_s_added")
        var_done, root_done = sem("var_done"), sem("root_done")
        diag_done, mdiag_done = sem("diag_done"), sem("mdiag_done")
        mr_ready = sem("mr_ready")
        loads_begun, turns_begun = sem("loads_begun"), sem("turns_begun")
        gains_ready, vec_ready = sem("gains_ready"), sem("vec_ready")
        dve_step = sem("dve_step")
        p_in_small, p_in_x, p_in_pos, p_const = sem("p_in_small"), sem("p_in_x"), sem("p_in_pos"), sem("p_const")
        p_pe, p_act, p_dve = sem("p_pe"), sem("p_act"), sem("p_dve")
        p_ang, p_sin = sem("p_angles"), sem("p_sines")
        y_ready, y_t, y_out, stored = sem("y_ready"), sem("y_turned"), sem("y_out"), sem("stored")

        class Chain:

            def __init__(self, eng, s):
                self.eng, self.s, self.n = eng, s, 0

            def __call__(self, ins):
                ins.then_inc(self.s, 1)
                self.n += 1

            def settle(self):
                if self.n:
                    self.eng.wait_ge(self.s, self.n)

            def restart(self):
                self.settle()
                if self.n:
                    self.eng.sem_clear(self.s)
                self.n = 0

        def layers(eng, body):
            with eng.Fori(0, DEPTH) as l:
                body(l)

        def chunks(eng, l, body):
            with eng.Fori(0, NC - 1) as c:
                body(l, c, False)
            body(l, NC - 1, True)

        def vcol(name, j=0, n=1, src=vec):
            at, _ = VEC[name]
            return vec[:, at + j:at + j + n]

        def acc_of(i, n=None):
            return acc[:, ACC_AT[i]:ACC_AT[i] + (i + 1) * P]

        def bias_of(i):
            return causal[:, (TT - 1) * P:] if i == 0 else acc_of(i)

        def pair_views(name, p):
            if name != "qi":
                return [(raw[:, p, :, :], w_hi[:, p, :, :], w_lo[:, p, :, :])]
            pieces = []
            for s in range(2):
                for head in range(2):
                    src = raw[:, p, s, :].rearrange("p (m head half d) -> p head m half d", m=4, head=2, half=2)[:, head]
                    hi, lo = (w[:, p, s, :].rearrange("p (m half head d) -> p head m half d", m=4, head=2, half=2)[:, head]
                              for w in (w_hi, w_lo))
                    pieces.append((src, hi, lo))
            return pieces

        block = ctx.enter_context(nc.Block())

        def load_first_mod(eng, n):
            eng.dma_start(first_mod[n][:, :, :], A["w_mod"][0, :, 2 * n * P:(2 * n + 2) * P]
                          .rearrange("(k p) n -> p k n", p=P)).then_inc(first_mod_in[n], 16)

        @block.sync
        def _(sp):
            sp.wait_ge(p_in_small, 16 * (len(VEC) + 1))
            for n in range(1, NEXT_PAIRS, 2):
                load_first_mod(sp, n)
                sp.dma_start(xs[:, n // 2, :], A["x"][0, n // 2 * P:(n // 2 + 1) * P, :]).then_inc(p_in_x, 16)

            def load_pair(src, l, name, p, c=None):
                g = group_at(name, l, c)
                sp.wait_ge(lo_split, g * PAIRS + (p + 1))
                sp.sem_inc(loads_begun, 1)
                sp.dma_start(raw[:, p, :, :], src).then_inc(raw_in[p], 16)

            def layer(l):
                for name in PRE[:6]:
                    for p in range(PAIRS):
                        load_pair(A["w_in"][l, 2 * p * P:(2 * p + 2) * P, COL[name]:COL[name] + T]
                                  .rearrange("(k p) n -> p k n", p=P), l, name, p)
                    if name == "qi":
                        sp.wait_ge(full_s[7], uses_before(7, "out13", l))
                        sp.wait_ge(p_pe, 1 + DK)
                        sp.sem_inc(loads_begun, 1)
                        sp.dma_start(kiwi_raw[:, :, :], A["w_in"][l, :, COL["kiwi"]:COL["kiwi"] + KIWI]
                                     .rearrange("(k p) n -> p k n", p=P)).then_inc(kiwi_in, 16)
                for j, name in enumerate(PRE[6:]):
                    for p in range(PAIRS):
                        row = OUT_ORDER[2 * p] * P
                        load_pair(A["w_out"][l, row:row + 2 * P, j * T:(j + 1) * T]
                                  .rearrange("(k p) n -> p k n", p=P), l, name, p)

                def chunk(l, c, last):
                    for j in range(2):
                        for p in range(PAIRS):
                            load_pair(A["w_up"][l, 2 * p * P:(2 * p + 2) * P, bass.ds(c * D + j * T, T)]
                                      .rearrange("(k p) n -> p k n", p=P), l, f"up{j}", p, c)
                    for j in range(2):
                        for p in range(PAIRS):
                            load_pair(A["w_down"][l, bass.ds(c * D + 2 * p * P, 2 * P), j * T:(j + 1) * T]
                                      .rearrange("(k p) n -> p k n", p=P), l, f"down{j}", p, c)
                chunks(sp, l, chunk)
            layers(sp, layer)
            for half in range(2):
                for n in range(TT):
                    sp.wait_ge(y_out, TT * half + n + 1)
                    sp.dma_start(out[0, n * P:(n + 1) * P, half * T:(half + 1) * T],
                                 xs[:, n, half * T:(half + 1) * T]).then_inc(stored, 16)
            sp.wait_ge(stored, 16 * 2 * TT)

        @block.gpsimd
        def _(pool):
            gp = nc.gpsimd
            gp.memset(ident[:, :], 0.0).then_inc(p_const, 1)
            gp.memset(causal[:, :], 0.0).then_inc(p_const, 1)
            pool.wait_ge(p_const, 2)
            gp.affine_select(out=ident[:, :], in_=ident[:, :], compare_op=ALU.not_equal, fill=1.0, base=0,
                             pattern=[[-1, P]], channel_multiplier=1).then_inc(p_const, 1)
            last_block = causal[:, (TT - 1) * P:]
            gp.affine_select(out=last_block, in_=last_block, compare_op=ALU.is_ge, fill=-BIG, base=0,
                             pattern=[[-1, P]], channel_multiplier=1).then_inc(p_const, 1)
            gp.memset(ident_d[:, :], 0.0).then_inc(p_const, 1)
            pool.wait_ge(p_const, 5)
            gp.affine_select(out=ident_d[:, :], in_=ident_d[:, :], compare_op=ALU.not_equal, fill=float(D), base=0,
                             pattern=[[-1, P]], channel_multiplier=1).then_inc(p_const, 1)
            gp.memset(ones_d[:, :], 1.0 / D).then_inc(p_const, 1)
            gp.memset(blk[:, :, :, :], 0.0).then_inc(p_const, 1)
            gp.memset(ki_a[:, :], 0.0).then_inc(p_const, 1)
            gp.memset(ki_b[:, :], 0.0).then_inc(p_const, 1)
            gp.memset(eps[:, :], LN_EPS).then_inc(p_const, 1)

            pool.wait_ge(p_in_small, 16 * (len(VEC) + 1))
            for n in range(0, NEXT_PAIRS, 2):
                load_first_mod(pool, n)
            pool.wait_ge(p_const, 11)

            def layer(l):
                pool.wait_ge(full_s[7], uses_before(7, "out13", l))
                for g, name in enumerate(("w_gate_a", "w_gate_x")):
                    for par in range(2):
                        pool.dma_start(blk[64 * par:64 * par + 64, g, :, 64 * par:64 * par + 64],
                                       A[name][l, :, :, :].rearrange("(t two) c d -> two c t d", two=2)[par])\
                            .then_inc(gate_in, 16)
                for n in range(LATE_PAIRS):
                    pool.wait_ge(mod_used, l * MOD_PAIRS + (NEXT_PAIRS + n + 1 - MR))
                    pool.dma_start(mod_raw[:, n % MR, :, :], A["w_mod"][l, :, (MODS_NEXT + 2 * n) * P:(MODS_NEXT + 2 * n + 2) * P]
                                   .rearrange("(k p) n -> p k n", p=P)).then_inc(mod_in[n % MR], 16)

                def sums(at):
                    for m in range(1, DK):
                        pool.wait_ge(ln_sq_s, at * DK + (m + 1))
                        if m > 1:
                            pool.wait_ge(ln_q_s, at * (DK - 1) + (1 + m))
                        gp.tensor_tensor(ln_q[:, :], ln_q[:, :], ln_sq[:, m % 2, :], ALU.add).then_inc(ln_q_s, 1)
                sums(l * 2)

                def chunk(l, c, last):
                    for n in range(2):
                        pool.wait_ge(mod_used, l * MOD_PAIRS + c * 2 + (NEXT_PAIRS + LATE_PAIRS + n + 1 - MR))
                        pool.dma_start(mod_raw[:, n, :, :], A["w_mod"][(l + 1) % DEPTH, :, bass.ds(c * T + 2 * n * P, 2 * P)]
                                       .rearrange("(k p) n -> p k n", p=P)).then_inc(mod_in[n], 16)
                chunks(pool, l, chunk)
                sums(l * 2 + 1)
            layers(pool, layer)

        @block.tensor
        def _(pe):
            mm = nc.tensor.matmul

            def turn(dst, src, idn):
                return nc.tensor.transpose(dst, src, idn)

            pe.wait_ge(p_const, 3)
            pe.wait_ge(p_in_small, 16 * (len(VEC) + 1))
            turn(banks[4][:, 0:P], stage[:, 0, :], ident[:, :])
            for l in range(1, DEPTH):
                last = turn(banks[4][:, l * P:l * P + NV], stage[0:NV, l, :], ident[0:NV, 0:NV])
            last.then_inc(p_pe, 1)
            def mod_pair(col, tiles):
                for s in range(2):
                    for kk in range(DK):
                        last = mm(banks[7][:, col + s:col + s + 1], tiles[:, kk, s * P:(s + 1) * P], csil[:, kk:kk + 1],
                                  start=(kk == 0), stop=(kk == DK - 1))
                last.then_inc(mod_used, 1)

            def summed_pair(col, tiles, count):
                pe.wait_ge(mod_sum, count)
                for s in range(2):
                    last = mm(banks[7][:, col + s:col + s + 1], tiles[:, 0, s * P:(s + 1) * P], ones_d[:, 0:1],
                              start=True, stop=True)
                last.then_inc(mod_used, 1)

            pe.wait_ge(p_dve, 1)
            pe.wait_ge(p_const, 11)
            for n in range(NEXT_PAIRS):
                if n % 2:
                    pe.wait_ge(first_mod_in[n], 16)
                    mod_pair(2 * n, first_mod[n])
            for n in range(0, NEXT_PAIRS, 2):
                summed_pair(2 * n, first_mod[n], n // 2 + 1)

            pe.wait_ge(p_in_x, 16 * TT)
            for m in range(DK):
                if m >= 4:
                    pe.wait_ge(p_act, m - 4 + 2)
                for n in range(TT):
                    last = turn(banks[m % 4][:, n * P:(n + 1) * P], xs[:, n, m * P:(m + 1) * P], ident[:, :])
                last.then_inc(p_pe, 1)

            def group(name, l, hi, lo, ready, c=None, order=range(DK), mods_before=None):
                set_ = bank_set(name)
                g = group_at(name, l, c)
                for p in range(PAIRS):
                    pe.wait_ge(lo_split, g * PAIRS + (PAIRS + p + 1))
                    steps = [(s, m) for s in range(2) for m in range(4)] if p < PAIRS - 1 else \
                        [(s, m) for m in range(4) for s in range(2)]
                    for s, m in steps:
                        kk = order[2 * p + s]
                        if m == 0:
                            ready(kk, 2 * p + s)
                        if p == 0 and s == 0:
                            pe.wait_ge(free_s[set_ + m], uses_before(set_ + m, f"{name}{m}", l, c))
                            if m == 3 and mods_before is not None:
                                pe.wait_ge(mods_out, mods_before)
                        wh, wl = (w[:, p, s, m * P:(m + 1) * P] for w in (w_hi, w_lo))
                        o = banks[set_ + m][:, :]
                        first, fin = p == 0 and s == 0, p == PAIRS - 1 and s == 1
                        mm(o, wh, hi[:, kk, :], start=first, stop=False)
                        mm(o, wh, lo[:, kk, :], start=False, stop=False)
                        last = mm(o, wl, hi[:, kk, :], start=False, stop=fin)
                        if fin:
                            last.then_inc(full_s[set_ + m], 1)
                    if p < PAIRS - 1:
                        last.then_inc(pair_used, 1)

            def a_ready(base):
                def wait(kk, n):
                    pe.wait_ge(a_lo_s, base + (2 + kk + 1))
                return wait

            def nothing(kk, n):
                pass

            def b_ready(base):
                def wait(kk, n):
                    pe.wait_ge(b_lo_s, base + (n + 1))
                return wait

            def idx_scores(i, l):
                for h in range(IDX_HEADS):
                    u = IDX.index((i, h))
                    b = 5 + u % 2
                    pe.wait_ge(rope_done, l * 13 + 5)
                    pe.wait_ge(free_s[b], uses_before(b, f"idx{u}", l))
                    mm(banks[b][:, 0:(i + 1) * P], qi[:, h // 2, i * P:(i + 1) * P],
                       (ki_b if h % 2 else ki_a)[:, 0:(i + 1) * P], start=True, stop=True).then_inc(full_s[b], 1)

            def spread(b, name, l, src):
                pe.wait_ge(free_s[b], uses_before(b, name, l))
                mm(banks[b][:, :], ones_d[:, :], src.rearrange("p t q -> p (t q)"), start=True, stop=True)\
                    .then_inc(full_s[b], 1)

            def layer_norm(l, tail, n):
                pe.wait_ge(ln_s_s, n)
                pe.wait_ge(free_s[4], uses_before(4, "sums" + tail, l))
                for t in range(TT):
                    mm(banks[4][:, t:t + 1], ln_s[:, t * P:(t + 1) * P], ones_d[:, 0:1], start=True, stop=True)
                pe.wait_ge(ln_q_s, n * (DK - 1) + 2)
                for t in range(TT):
                    last = mm(banks[4][:, TT + t:TT + t + 1], ln_q[:, t * P:(t + 1) * P], ones_d[:, 0:1], start=True, stop=True)
                last.then_inc(full_s[4], 1)
                pe.wait_ge(diag_done, l * 4 + (4 if tail else 3))
                spread(4, "rb" + tail, l, diag[:, 0])
                pe.wait_ge(mdiag_done, n)
                spread(5, "mb" + tail, l, diag[:, 1])

            def layer(l):
                def late_mod(n):
                    if n == 0:
                        pe.wait_ge(free_s[7], uses_before(7, "out13", l))
                        pe.wait_ge(mods_out, l * (NC + 1) + 1)
                    pe.wait_ge(mod_in[n % MR], l * (16 * MOD_PAIRS // MR) + 16 * (n // MR + 1))
                    row, o = n // 2, banks[7][0:MOD_ROWS, n % 2 * 2 * P:(n % 2 + 1) * 2 * P]
                    for kk in range(DK):
                        last = mm(o, csil_w[:, kk, MOD_ROWS - 1 - row:2 * MOD_ROWS - 1 - row], mod_raw[:, n % MR, kk, :],
                                  start=(n == 0 and kk == 0), stop=(n == LATE_PAIRS - 1 and kk == DK - 1))
                    last.then_inc(mod_used, 1)

                def turn_mods():
                    pe.wait_ge(mod_rows_s, l + 1)
                    pe.sem_inc(turns_begun, 1)
                    for t in range(TT):
                        last = turn(banks[7][:, t * MOD_ROWS:(t + 1) * MOD_ROWS], mod_rows[:, t * P:(t + 1) * P],
                                    ident[0:MOD_ROWS, 0:MOD_ROWS])
                    last.then_inc(mods_turned, 1)

                group("qi", l, a_hi, a_lo, a_ready(l * 2 * DK))
                late_mod(0)
                pe.wait_ge(kiwi_lo_s, l + 1)
                pe.wait_ge(free_s[4], uses_before(4, "kiwi", l))
                for kk in range(DK):
                    o = banks[4][0:KIWI, :]
                    mm(o, kiwi_hi[:, kk, :], a_hi[:, kk, :], start=(kk == 0), stop=False)
                    mm(o, kiwi_hi[:, kk, :], a_lo[:, kk, :], start=False, stop=False)
                    last = mm(o, kiwi_lo[:, kk, :], a_hi[:, kk, :], start=False, stop=(kk == DK - 1))
                last.then_inc(full_s[4], 1)
                group("xr", l, a_hi, a_lo, nothing)
                late_mod(1)
                pe.wait_ge(free_s[4], uses_before(4, "kiwi", l) + 1)
                pe.wait_ge(free_s[4], uses_before(4, "wi", l))
                pe.sem_inc(turns_begun, 1)
                for n in range(TT):
                    last = turn(banks[4][:, n * IDX_HEADS:(n + 1) * IDX_HEADS], rraw[64:64 + IDX_HEADS, 0, n * P:(n + 1) * P],
                                ident[64:64 + IDX_HEADS, 64:64 + IDX_HEADS])
                last.then_inc(full_s[4], 1)
                idx_scores(1, l)
                group("yg", l, a_hi, a_lo, nothing)
                idx_scores(2, l)
                late_mod(2)
                group("v", l, a_hi, a_lo, nothing)
                idx_scores(3, l)
                late_mod(3)
                for m in range(HEADS):
                    pe.wait_ge(free_s[m], uses_before(m, f"v{m}", l) + 1)
                    pe.wait_ge(free_s[4], uses_before(4, f"vt{m}", l))
                    for n in range(TT):
                        last = turn(banks[4][:, n * P:(n + 1) * P], rraw[:, (5 + m) % 2, n * P:(n + 1) * P], ident[:, :])
                    last.then_inc(full_s[4], 1)
                group("k", l, a_hi, a_lo, nothing)
                late_mod(4)
                group("q", l, a_hi, a_lo, nothing)
                late_mod(5)
                pe.wait_ge(gate_in, l * 64 + 64)
                for m in range(LT):
                    pe.wait_ge(conv_done, l * LT + (m + 1))
                    for g, (b, name) in enumerate(((4, f"gr{m}"), (5, f"gi{m}"))):
                        pe.wait_ge(free_s[b], uses_before(b, name, l))
                        mm(banks[b][:, :], blk[:, g, m, :], xc[:, m, :], start=True, stop=True).then_inc(full_s[b], 1)

                def scores(u):
                    i, h = UNITS[u]
                    b = 5 + u % 2
                    pe.wait_ge(free_s[b], uses_before(b, f"s{u}", l))
                    mm(banks[b][:, 0:(i + 1) * P], q[:, h, i * P:(i + 1) * P], k[:, h, 0:(i + 1) * P],
                       start=True, stop=True).then_inc(full_s[b], 1)

                def turned(u):
                    i, h = UNITS[u]
                    b = 2 + u % 2
                    pe.wait_ge(attn_p, l * 16 + (u + 1))
                    pe.wait_ge(free_s[b], uses_before(b, f"pt{u}", l))
                    for j in range(i + 1):
                        last = turn(banks[b][:, j * P:(j + 1) * P], probs[:, u % 4, j * P:(j + 1) * P], ident[:, :])
                    last.then_inc(full_s[b], 1)

                def values(u):
                    i, h = UNITS[u]
                    b = i % 2
                    pe.wait_ge(free_s[2 + u % 2], uses_before(2 + u % 2, f"pt{u}", l) + 1)
                    if h == 0:
                        pe.wait_ge(free_s[b], uses_before(b, f"o{i}", l))
                    for j in range(i + 1):
                        last = mm(banks[b][:, h * P:(h + 1) * P], v[:, j, h * DH:(h + 1) * DH],
                                  probs_t[:, u % 2, j * P:(j + 1) * P], start=(j == 0), stop=(j == i))
                    last.then_inc(full_s[b] if h == HEADS - 1 else pv_done, 1)

                late_mod(6)
                pe.wait_ge(rope_done, l * 13 + 13)
                pe.wait_ge(free_s[4], uses_before(4, f"vt{HEADS - 1}", l) + 1)
                scores(0)
                scores(1)
                for u in range(len(UNITS)):
                    if u + 2 < len(UNITS):
                        scores(u + 2)
                    if u + 7 < LATE_PAIRS:
                        late_mod(u + 7)
                    turned(u)
                    if u >= 1:
                        values(u - 1)
                values(len(UNITS) - 1)
                pe.wait_ge(sq_ready, l * LT + LT)
                pe.wait_ge(free_s[4], uses_before(4, "lms", l))
                for t in range(TT):
                    for m in range(LT):
                        last = mm(banks[4][:, t:t + 1], sq_l[:, m, t * P:(t + 1) * P], ones_d[:, 0:1],
                                  start=(m == 0), stop=(m == LT - 1))
                last.then_inc(full_s[4], 1)
                pe.wait_ge(free_s[5], uses_before(5, "ams", l))
                for i in range(TT):
                    pe.wait_ge(free_s[i % 2], uses_before(i % 2, f"o{i}", l) + 1)
                    for h in range(HEADS):
                        last = mm(banks[5][:, i:i + 1], sq_a[:, i, h * P:(h + 1) * P], ones_d[:, 0:1],
                                  start=(h == 0), stop=(h == HEADS - 1))
                last.then_inc(full_s[5], 1)
                for n, (b, name, src) in enumerate(((4, "lrb", diag_l), (5, "arb", diag_a))):
                    pe.wait_ge(diag_done, l * 4 + (n + 1))
                    spread(b, name, l, src)

                group("out0", l, b_hi, b_lo, b_ready(l * (5 * DK)), order=OUT_ORDER)
                turn_mods()
                group("out1", l, b_hi, b_lo, nothing, order=OUT_ORDER, mods_before=l * (NC + 1) + 2)
                layer_norm(l, "", l * 2 + 1)

                def chunk(l, c, last):
                    group("up0", l, a_hi, a_lo, a_ready(l * 2 * DK + DK), c)
                    pe.wait_ge(free_s[7], uses_before(7, "up13", l, c))
                    for n in range(2):
                        summed_pair(2 * n, mod_raw[:, n, :, :],
                                    l * NEXT_PAIRS + c * 2 + (NEXT_PAIRS // 2 + n + 1))
                    group("up1", l, a_hi, a_lo, nothing, c, mods_before=l * (NC + 1) + c + 3)
                    group("down0", l, b_hi, b_lo, b_ready(l * (5 * DK) + DK + c * DK), c)
                    group("down1", l, b_hi, b_lo, nothing, c)
                chunks(pe, l, chunk)
                layer_norm(l, "_b", l * 2 + 2)
            layers(pe, layer)

            for m in range(DK):
                pe.wait_ge(y_ready, m + 1)
                for n in range(TT):
                    b = 4 * (m // 4) + n
                    last = turn(banks[b][:, (m % 4) * P:(m % 4 + 1) * P], x[:, m, n * P:(n + 1) * P], ident[:, :])
                    if m % 4 == 3:
                        last.then_inc(y_t, 1)

        @block.scalar
        def _(act):
            af = nc.scalar.activation

            for name, (at, n) in VEC.items():
                src = A[name]
                if name == "conv_w":
                    src = src.rearrange("l j (t p) -> (j t) l p", p=P)
                else:
                    src = src.rearrange("l (t p) -> t l p", p=P)
                act.dma_start(stage[at:at + n, :, :], src).then_inc(p_in_small, 16)
            act.dma_start(stage[NV:P, 0, :], A["c"].rearrange("b (t p) -> (b t) p", p=P)).then_inc(p_in_small, 16)
            act.dma_start(pos[:, :], A["positions"][0:1, :].broadcast_to([P, T])).then_inc(p_in_pos, 16)
            act.dma_start(freq[:, :], A["freq"]).then_inc(p_in_pos, 16)
            act.wait_ge(p_pe, 1)
            for l in range(DEPTH):
                n = P if l == 0 else NV
                last = af(vecs[:, l, 0:n], banks[4][:, l * P:l * P + n], ACT.Copy)
            last.then_inc(p_act, 1)
            act.wait_ge(p_act, 1)
            af(csil[:, :], vecs[:, 0, NV:P], ACT.Sigmoid).then_inc(p_sin, 1)
            at, n = VEC["lru_lambda"]
            af(spt[:, 0, :, :], vecs[:, :, at:at + n], ACT.Abs).then_inc(p_sin, 1)
            act.wait_ge(p_sin, 2)
            af(spt[:, 0, :, :], spt[:, 0, :, :], ACT.Exp, scale=-1.0).then_inc(p_sin, 1)
            for m in range(DK):
                act.wait_ge(p_pe, m + 2)
                af(x[:, m, :], banks[m % 4][:, :], ACT.Copy).then_inc(p_act, 1)
            act.wait_ge(p_ang, 1)
            for dst, src in ((sin_m, 0), (sin_i, 1), (cos_m, 2), (cos_i, 3)):
                af(dst[:, :], ang[:, src, :], ACT.Sin).then_inc(p_sin, 1)

            def split_hi(name, l, p, c=None):
                g = group_at(name, l, c)
                act.wait_ge(raw_in[p], 16 * (g + 1))
                if p < PAIRS - 1:
                    act.wait_ge(pair_used, g * (PAIRS - 1) + (p + 1))
                elif name == "qi":
                    act.wait_ge(full_s[7], uses_before(7, "out13", l))
                elif name == "up0":
                    act.wait_ge(full_s[7], uses_before(7, "up13", l, c))
                else:
                    names = CHUNK if c is not None else PRE
                    prev = names[names.index(name) - 1]
                    b = bank_set(prev) + 3
                    act.wait_ge(full_s[b], uses_before(b, f"{prev}3", l, c) + 1)
                for src, hi, _ in pair_views(name, p):
                    last = af(hi, src, ACT.Copy)
                last.then_inc(hi_split, 1)

            def a_tile(l, blk, kk):
                n = l * 2 * DK + (blk * DK + kk)
                g, b = gains[:, 4 * blk, kk:kk + 1], gains[:, 4 * blk + 1, kk:kk + 1]
                act.wait_ge(xn_ready, n + 1)
                act.wait_ge(a_lo_s, n + 1)
                af(full[:, kk % 2, :], x[:, kk, :], ACT.Identity, bias=b, scale=g)
                af(a_hi[:, kk, :], x[:, kk, :], ACT.Identity, bias=b, scale=g).then_inc(a_hi_s, 1)

            def scale_residual(blk):
                for kk in range(DK):
                    af(x[:, kk, :], x[:, kk, :], ACT.Identity, bias=gains[:, 4 * blk + 3, kk:kk + 1],
                       scale=gains[:, 4 * blk + 2, kk:kk + 1]).then_inc(x_scaled, 1)

            def slot(l, nxt, takeout, c=None, nc_=None):
                for p in range(PAIRS - 1):
                    split_hi(nxt, l, p, c if nc_ is None else nc_)
                takeout()
                split_hi(nxt, l, PAIRS - 1, c if nc_ is None else nc_)

            def ln_squares(l, base, ms, name, c=None):
                for m in ms:
                    b = bank_set(name) + m % 4
                    act.wait_ge(free_s[b], uses_before(b, f"{name}{m % 4}", l, c) + 1)
                    if m:
                        act.wait_ge(ln_q_s, base * (DK - 1) + m)
                    af(ln_sq[:, m % 2, :] if m else ln_q[:, :], x[:, m, :], ACT.Square).then_inc(ln_sq_s, 1)

            def root(n):
                act.wait_ge(var_done, n)
                af(stat[:, 2, :], stat[:, 2, :], ACT.Sqrt).then_inc(root_done, 1)

            def norm_out(l, tail, n):
                root(n)
                act.wait_ge(mr_ready, l * 2 + (2 if tail else 1))
                for t in range(TT):
                    last = af(diag[:, 1, t, :], ident_d[:, :], ACT.Copy, scale=stat[:, 4, t:t + 1])
                last.then_inc(mdiag_done, 1)
                for b, name, dst in ((4, "rb", rstd), (5, "mb", mrstd)):
                    act.wait_ge(full_s[b], uses_before(b, name + tail, l) + 1)
                    af(dst[:, :], banks[b][:, :], ACT.Copy).then_inc(free_s[b], 1)

            def layer(l):
                split_hi("qi", l, 0)
                split_hi("qi", l, 1)
                act.wait_ge(gains_ready, l * 2 + 1)
                for kk in range(DK):
                    a_tile(l, 0, kk)
                    if kk == 1:
                        split_hi("qi", l, 2)
                    if kk == 3:
                        split_hi("qi", l, 3)
                act.wait_ge(kiwi_in, 16 * (l + 1))
                af(kiwi_hi[:, :, :], kiwi_raw[:, :, :], ACT.Copy).then_inc(kiwi_hi_s, 1)
                scale_residual(0)

                def ring_free(t):
                    t -= 2
                    if 5 <= t < 9:
                        act.wait_ge(full_s[4], uses_before(4, f"vt{t - 5}", l) + 1)
                    elif t >= 0:
                        act.wait_ge(rope_done, l * 13 + (t + 1 if t < 5 else t - 3))

                def rope_tile(name, t, m):
                    b = m
                    ring_free(t)
                    act.wait_ge(full_s[b], uses_before(b, f"{name}{m}", l) + 1)
                    af(rraw[:, t % 2, :], banks[b][:, :], ACT.Copy)
                    af(rrot[0:64, t % 2, :], banks[b][64:P, :], ACT.Copy)
                    af(rrot[64:P, t % 2, :], banks[b][0:64, :], ACT.Copy).then_inc(free_s[b], 1)

                def qi_out():
                    for m in range(4):
                        rope_tile("qi", m, m)
                act.wait_ge(vec_ready, l + 1)
                slot(l, "xr", qi_out)
                ring_free(4)
                act.wait_ge(full_s[4], uses_before(4, "kiwi", l) + 1)
                af(rraw[0:KIWI, 0, :], banks[4][0:KIWI, :], ACT.Copy)
                af(rrot[0:32, 0, :], banks[4][32:64, :], ACT.Copy)
                af(rrot[32:64, 0, :], banks[4][0:32, :], ACT.Copy).then_inc(free_s[4], 1)

                def xr_out():
                    for m in range(LT):
                        act.wait_ge(full_s[m], uses_before(m, f"xr{m}", l) + 1)
                        af(xr[:, m, CONV - 1:], banks[m][:, :], ACT.Copy).then_inc(free_s[m], 1)
                slot(l, "yg", xr_out)
                act.wait_ge(full_s[4], uses_before(4, "wi", l) + 1)
                af(wi[:, :, :].rearrange("p t h -> p (t h)"), banks[4][:, 0:TT * IDX_HEADS], ACT.Copy,
                   scale=IDX_HEADS ** -0.5).then_inc(free_s[4], 1)

                def idx_relu(i):
                    if i == 1:
                        act.wait_ge(a_lo_s, l * 2 * DK + (DK + 2))
                    for h in range(IDX_HEADS):
                        u = IDX.index((i, h))
                        b = 5 + u % 2
                        act.wait_ge(full_s[b], uses_before(b, f"idx{u}", l) + 1)
                        act.wait_ge(idx_acc, l * len(IDX) + (u + 1))
                        af(rel[:, u % 2, 0:(i + 1) * P], banks[b][:, 0:(i + 1) * P], ACT.Relu).then_inc(free_s[b], 1)
                idx_relu(1)

                def yg_out():
                    for m in range(LT):
                        act.wait_ge(full_s[m], uses_before(m, f"yg{m}", l) + 1)
                        af(yg[:, m, :], banks[m][:, :], ACT.Gelu_apprx_tanh).then_inc(free_s[m], 1)
                slot(l, "v", yg_out)
                idx_relu(2)

                def v_out_first():
                    for m in range(2):
                        v_copy(m)

                def v_copy(m):
                    ring_free(5 + m)
                    act.wait_ge(full_s[m], uses_before(m, f"v{m}", l) + 1)
                    af(rraw[:, (5 + m) % 2, :], banks[m][:, :], ACT.Copy).then_inc(free_s[m], 1)

                def v_out():
                    for m in range(2, HEADS):
                        vt_out(m - 2)
                        v_copy(m)
                    vt_out(HEADS - 2)

                def vt_out(m):
                    if m < 0:
                        return
                    act.wait_ge(full_s[4], uses_before(4, f"vt{m}", l) + 1)
                    af(v[:, :, m * DH:(m + 1) * DH], banks[4][:, :].rearrange("p (t d) -> p t d", t=TT),
                       ACT.Copy).then_inc(free_s[4], 1)
                for p in range(PAIRS):
                    split_hi("k", l, p)
                    if p == PAIRS - 2:
                        v_out_first()
                idx_relu(3)
                v_out()
                vt_out(HEADS - 1)

                def k_out():
                    for m in range(HEADS):
                        rope_tile("k", 9 + m, m)
                slot(l, "q", k_out)

                def q_out():
                    for m in range(HEADS):
                        rope_tile("q", 13 + m, m)
                slot(l, "out0", q_out)
                for m in range(LT):
                    for b, name, dst, bias in ((4, "gr", th, "b_gate_a"), (5, "gi", gi, "b_gate_x")):
                        act.wait_ge(full_s[b], uses_before(b, f"{name}{m}", l) + 1)
                        af(dst[:, m, :], banks[b][:, :], ACT.Sigmoid, bias=vcol(bias, m)).then_inc(free_s[b], 1)
                for m in range(LT):
                    act.wait_ge(free_s[4], uses_before(4, f"gr{m}", l) + 1)
                    af(lru_a[:, m, :], th[:, m, :], ACT.Exp, scale=neg_sp[:, m:m + 1])
                    af(th[:, m, :], th[:, m, :], ACT.Tanh, scale=vcol("lru_lambda", m)).then_inc(lru_exp, 1)

                def expo(u):
                    i, h = UNITS[u]
                    act.wait_ge(attn_max, l * 16 + (u + 1))
                    pr = probs[:, u % 4, 0:(i + 1) * P]
                    af(pr, pr, ACT.Exp, bias=negm[:, u:u + 1], scale=SCALE, accum_out=rsum[:, u:u + 1]).then_inc(attn_exp, 1)

                def probs_turned(u):
                    i, h = UNITS[u]
                    b = 2 + u % 2
                    act.wait_ge(full_s[b], uses_before(b, f"pt{u}", l) + 1)
                    if u >= 2:
                        i2, h2 = UNITS[u - 2]
                        if h2 == HEADS - 1:
                            act.wait_ge(full_s[i2 % 2], uses_before(i2 % 2, f"o{i2}", l) + 1)
                        else:
                            act.wait_ge(pv_done, l * 12 + (3 * i2 + h2 + 1))
                    n = (i + 1) * P
                    af(probs_t[:, u % 2, 0:n], banks[b][:, 0:n], ACT.Copy).then_inc(free_s[b], 1)

                def attn_tile_out(i):
                    b = i % 2
                    act.wait_ge(full_s[b], uses_before(b, f"o{i}", l) + 1)
                    af(ao[:, :, i * P:(i + 1) * P], banks[b][:, :].rearrange("p (h q) -> p h q", h=HEADS), ACT.Copy)
                    af(sq_a[:, i, :], banks[b][:, :], ACT.Square).then_inc(free_s[b], 1)

                for u in range(len(UNITS)):
                    expo(u)
                    if u >= 1:
                        probs_turned(u - 1)
                    if u >= 6 and (u - 2) % HEADS == 0:
                        attn_tile_out((u - 2) // HEADS - 1)
                    if u == 5:
                        for m in range(LT):
                            act.wait_ge(lru_m, l * LT + (m + 1))
                            af(th[:, m, :], th[:, m, :], ACT.Sqrt).then_inc(lru_sqrt, 1)
                    if u >= 12:
                        m = u - 12
                        act.wait_ge(lru_out, l * LT + (m + 1))
                        af(sq_l[:, m, :], xc[:, m, :], ACT.Square).then_inc(sq_ready, 1)
                probs_turned(len(UNITS) - 1)
                attn_tile_out(TT - 1)
                root(l * 4 + 1)
                root(l * 4 + 2)
                act.wait_ge(mod_used, l * MOD_PAIRS + (NEXT_PAIRS + LATE_PAIRS))
                af(mod_rows[:, :], banks[7][0:MOD_ROWS, :], ACT.Copy).then_inc(mod_rows_s, 1)
                for n, kk in enumerate(OUT_ORDER):
                    act.wait_ge(m_full, l * DK + (n + 2))
                    af(b_hi[:, kk, :], full[:, n % 2, :], ACT.Copy).then_inc(b_hi_s, 1)

                def out_out(j):
                    def run():
                        ln_squares(l, l * 2, range(4 * j, 4 * j + 4), f"out{j}")
                    return run
                slot(l, "out1", out_out(0))
                slot(l, "up0", out_out(1), nc_=0)
                norm_out(l, "", l * 4 + 3)
                act.wait_ge(gains_ready, l * 2 + 2)
                for kk in range(DK):
                    a_tile(l, 1, kk)
                scale_residual(1)

                def chunk(l, c, last):
                    def hidden(j):
                        def hi(t):
                            act.wait_ge(ff_sq, l * (NC * DK) + c * DK + (2 + t + 1))
                            if t == 0:
                                act.wait_ge(full_s[7], uses_before(7, "up13", l, c))
                            af(b_hi[:, t, :], ffsq[:, t % 2, :], ACT.Copy).then_inc(b_hi_s, 1)

                        def run():
                            for m in range(4):
                                t = 4 * j + m
                                b = bank_set(f"up{j}") + m
                                act.wait_ge(full_s[b], uses_before(b, f"up{j}{m}", l, c) + 1)
                                act.wait_ge(ff_sq, l * (NC * DK) + c * DK + (t + 1))
                                af(relu[:, t % 2, :], banks[b][:, :], ACT.Relu).then_inc(free_s[b], 1)
                                if m:
                                    hi(t - 1)
                            hi(4 * j + 3)
                        return run
                    slot(l, "up1", hidden(0), c)
                    slot(l, "down0", hidden(1), c)
                    if not last:
                        slot(l, "down1", lambda: None, c)
                        slot(l, "up0", lambda: None, c + 1)
                    else:
                        base = l * 2 + 1
                        slot(l, "down1", lambda: ln_squares(l, base, range(4), "down0", c), c)
                        ln_squares(l, base, range(4, 8), "down1", c)
                chunks(act, l, chunk)
                norm_out(l, "_b", l * 4 + 4)
            layers(act, layer)

            def y_tiles(half):
                for n in range(TT):
                    act.wait_ge(y_t, TT * half + n + 1)
                    af(xs[:, n, half * T:(half + 1) * T], banks[4 * half + n][:, :], ACT.Copy).then_inc(y_out, 1)

            for m in range(DK):
                act.wait_ge(xn_ready, DEPTH * 2 * DK + (m + 1))
                af(x[:, m, :], x[:, m, :], ACT.Identity, bias=vcol("ln2_b", m), scale=vcol("ln2_g", m)).then_inc(y_ready, 1)
                if m == 5:
                    y_tiles(0)
            y_tiles(1)

        @block.vector
        def _(ve):
            v_ = nc.vector
            step = Chain(ve, dve_step)
            tt, ts, stt = v_.tensor_tensor, v_.tensor_scalar, v_.scalar_tensor_tensor

            for s in full_s + free_s + [m_full]:
                ve.sem_inc(s, 1)
            ve.sem_inc(lo_split, PAIRS)
            ve.sem_inc(pair_used, PAIRS - 1)
            ve.sem_inc(a_lo_s, 2)
            ve.sem_inc(ff_sq, 2)
            ve.sem_inc(idx_acc, 2)
            ve.sem_inc(ln_q_s, 2)
            step(v_.memset(mrstd[:, :], 0.0))
            step(v_.memset(rstd[:, :], 1.0))
            step(v_.memset(gains[:, 4:6, :], 1.0))
            step(v_.memset(csil_w[:, :, :], 0.0))
            step.settle()
            ve.wait_ge(p_sin, 1)
            tt(csil[:, :], csil[:, :], vecs[:, 0, NV:P], ALU.mult).then_inc(p_dve, 1)
            ve.wait_ge(p_dve, 1)
            step(v_.tensor_copy(csil_w[:, :, MOD_ROWS - 1], csil[:, :]))
            step(ts(csil_d[:, :], csil[:, :], float(D), None, ALU.mult))
            ve.wait_ge(p_sin, 3)
            e, z, z2, s_ = (spt[:, n, :, :] for n in range(4))
            at, n = VEC["lru_lambda"]
            lam = vecs[:, :, at:at + n]
            step(ts(z, e, 2.0, None, ALU.add))
            step.settle()
            step(v_.reciprocal(z, z))
            step.settle()
            step(tt(z, z, e, ALU.mult))
            step.settle()
            step(tt(z2, z, z, ALU.mult))
            step.settle()
            step(ts(s_, z2, 1.0 / 17, None, ALU.mult))
            for odd in range(15, 1, -2):
                step.settle()
                step(stt(s_, s_, 1.0 / odd, z2, ALU.add, ALU.mult))
            step.settle()
            step(stt(s_, s_, 1.0, z, ALU.add, ALU.mult))
            step(ts(lam, lam, -1.0, 0.0, ALU.mult, ALU.max))
            step.settle()
            step(stt(lam, s_, 2.0, lam, ALU.mult, ALU.add))
            step.settle()
            step(ts(lam, lam, LRU_C, None, ALU.mult))
            ve.wait_ge(p_in_pos, 32)
            step(v_.tensor_copy(posf[:, :], pos[:, :]))
            step.settle()
            for n in range(2):
                step(ts(ang[:, n, :], posf[:, :], freq[:, n:n + 1], None, ALU.mult))
            step.settle()
            for n in range(2):
                step(ts(ang[:, 2 + n, :], ang[:, n, :], 1.0 / (2 * np.pi), ROUND, ALU.mult, ALU.add))
            step.settle()
            for n in range(2):
                step(ts(ang[:, 2 + n, :], ang[:, 2 + n, :], -ROUND, None, ALU.add))
            for part in TWO_PI:
                step.settle()
                for n in range(2):
                    step(stt(ang[:, n, :], ang[:, 2 + n, :], -part, ang[:, n, :], ALU.mult, ALU.add))
            step.settle()
            for n in range(2):
                step(ts(ang[:, n, :], ang[:, n, :], PI_IN, -PI_IN, ALU.min, ALU.max))
            step.settle()
            for n in range(2):
                step(stt(ang[:, 2 + n, :], ang[:, n, :], -1.0, ang[:, n, :], ALU.mult, ALU.min))
            step.settle()
            for n in range(2):
                step(ts(ang[:, 2 + n, :], ang[:, 2 + n, :], float(np.pi / 2), None, ALU.add))
            step.settle()
            ve.sem_inc(p_ang, 1)

            def next_gains(l_next, g_prev, b_prev):
                at, _ = VEC["b_mod"]
                step(tt(modn[:, :].rearrange("p (one n) -> p one n", one=1),
                        modn[:, :].rearrange("p (one n) -> p one n", one=1),
                        vecs[:, bass.ds(l_next, 1), at:at + MODS_NEXT], ALU.add))
                step.settle()
                fold_gains(0, modn[:, 0:DK], modn[:, DK:2 * DK], g_prev, b_prev)

            def fold_gains(blk, shift, scale, g, b):
                G, B, RG, RB = (gains[:, 4 * blk + n, :] for n in range(4))
                step(ts(RG, g, ALPHA, None, ALU.mult))
                step(ts(RB, b, ALPHA, None, ALU.mult))
                step(stt(G, scale, 1.0, g, ALU.add, ALU.mult))
                step(stt(B, scale, 1.0, b, ALU.add, ALU.mult))
                step.settle()
                tt(B, B, shift, ALU.add).then_inc(gains_ready, 1)

            def weigh(tiles):
                step(ts(tiles[:, 0, :], tiles[:, 0, :], csil_d[:, 0:1], None, ALU.mult))
                for kk in range(1, DK):
                    step.settle()
                    ins = stt(tiles[:, 0, :], tiles[:, kk, :], csil_d[:, kk:kk + 1], tiles[:, 0, :], ALU.mult, ALU.add)
                    if kk == DK - 1:
                        ins.then_inc(mod_sum, 1)
                    else:
                        step(ins)

            for n in range(0, NEXT_PAIRS, 2):
                ve.wait_ge(first_mod_in[n], 16)
                weigh(first_mod[n])
            ve.wait_ge(mod_used, NEXT_PAIRS)
            v_.tensor_copy(modn[:, :], banks[7][:, 0:MODS_NEXT]).then_inc(mods_out, 1)
            ve.wait_ge(mods_out, 1)
            step(v_.memset(gains[:, 5, :], 0.0))
            step.settle()
            next_gains(0, gains[:, 4, :], gains[:, 5, :])
            ve.wait_ge(p_act, 1 + DK)
            ve.wait_ge(p_const, 11)
            step.restart()

            def split_lo(name, l, p, c=None):
                g = group_at(name, l, c)
                ve.wait_ge(hi_split, g * PAIRS + (p + 1))
                for src, hi, lo in pair_views(name, p):
                    last = tt(lo, src, hi.bitcast(F32), ALU.subtract)
                last.then_inc(lo_split, 1)

            def norm_tile(kk):
                xk = x[:, kk, :]
                step(tt(xk, xk, rstd[:, :], ALU.mult))
                step.settle()
                tt(xk, xk, mrstd[:, :], ALU.subtract).then_inc(xn_ready, 1)

            def a_lo_tile(l, blk, kk):
                ve.wait_ge(a_hi_s, l * 2 * DK + (blk * DK + kk + 1))
                tt(a_lo[:, kk, :], full[:, kk % 2, :], a_hi[:, kk, :].bitcast(F32), ALU.subtract).then_inc(a_lo_s, 1)

            def per_token(n, dst):
                ve.wait_ge(root_done, n)
                step(v_.reciprocal(stat[:, 3, :], stat[:, 2, :]))
                step.settle()
                for t in range(TT):
                    last = ts(dst[:, t, :], ident_d[:, :], stat[:, 3, t:t + 1], None, ALU.mult)
                last.then_inc(diag_done, 1)

            def mean_square(l, b, name, width):
                ve.wait_ge(full_s[b], uses_before(b, name, l) + 1)
                step(ts(stat[:, 2, :], banks[b][:, 0:TT], D / width, LN_EPS, ALU.mult, ALU.add))
                step.settle()
                ve.sem_inc(free_s[b], 1)
                ve.sem_inc(var_done, 1)

            def ln_stats(l, tail, n):
                ve.wait_ge(full_s[4], uses_before(4, "sums" + tail, l) + 1)
                v_.tensor_copy(stat[:, 0:2, :].rearrange("p a t -> p (a t)"), banks[4][:, 0:2 * TT]).then_inc(free_s[4], 1)
                ve.wait_ge(free_s[4], uses_before(4, "sums" + tail, l) + 1)
                step(tt(stat[:, 2, :], stat[:, 0, :], stat[:, 0, :], ALU.mult))
                step.settle()
                step(tt(stat[:, 2, :], stat[:, 1, :], stat[:, 2, :], ALU.subtract))
                step.settle()
                ts(stat[:, 2, :], stat[:, 2, :], 0.0, LN_EPS, ALU.max, ALU.add).then_inc(var_done, 1)
                ve.wait_ge(root_done, n)
                step(v_.reciprocal(stat[:, 3, :], stat[:, 2, :]))
                step.settle()
                tt(stat[:, 4, :], stat[:, 0, :], stat[:, 3, :], ALU.mult).then_inc(mr_ready, 1)
                for t in range(TT):
                    last = ts(diag[:, 0, t, :], ident_d[:, :], stat[:, 3, t:t + 1], None, ALU.mult)
                last.then_inc(diag_done, 1)
                ve.wait_ge(free_s[4], uses_before(4, "rb" + tail, l) + 1)
                ve.wait_ge(free_s[5], uses_before(5, "mb" + tail, l) + 1)
                ve.sem_inc(dve_step, 1)
                step.n += 1

            def residual(l, name, m, gate, c=None):
                b = bank_set(name) + m % 4
                ve.wait_ge(full_s[b], uses_before(b, f"{name}{m % 4}", l, c) + 1)
                stt(x[:, m, :], banks[b][:, :], mods[:, gate * DK + m:gate * DK + m + 1], x[:, m, :],
                    ALU.mult, ALU.add).then_inc(free_s[b], 1)

            def ln_sum(l, name, m, c=None):
                b = bank_set(name) + m % 4
                ve.wait_ge(free_s[b], uses_before(b, f"{name}{m % 4}", l, c) + 1)
                if m == 0:
                    step(v_.tensor_copy(ln_s[:, :], x[:, 0, :]))
                else:
                    step.settle()
                    ins = tt(ln_s[:, :], ln_s[:, :], x[:, m, :], ALU.add)
                    if m == DK - 1:
                        ins.then_inc(ln_s_s, 1)
                    else:
                        step(ins)

            def slot(l, nxt, work, c=None, nc_=None):
                cn = c if nc_ is None else nc_
                for p in range(PAIRS - 1):
                    split_lo(nxt, l, p, cn)
                    work[p]()
                split_lo(nxt, l, PAIRS - 1, cn)

            def none():
                pass

            def layer(l):
                norm_tile(0)
                split_lo("qi", l, 0)
                for kk in range(1, DK):
                    norm_tile(kk)
                    a_lo_tile(l, 0, kk - 1)
                    if kk in (2, 4, 5):
                        split_lo("qi", l, (2, 4, 5).index(kk) + 1)
                a_lo_tile(l, 0, DK - 1)
                step(v_.memset(xr[:, :, 0:CONV - 1], 0.0))
                step(v_.tensor_copy(vec[:, :].rearrange("p (one n) -> p one n", one=1), vecs[:, bass.ds(l, 1), 0:NV]))
                ve.wait_ge(kiwi_hi_s, l + 1)
                tt(kiwi_lo[:, :, :], kiwi_raw[:, :, :], kiwi_hi[:, :, :].bitcast(F32), ALU.subtract).then_inc(kiwi_lo_s, 1)
                step.settle()
                step(ts(neg_sp[:, :], vcol("lru_lambda", 0, LT), -1.0, None, ALU.mult))
                step.settle()
                ve.sem_inc(vec_ready, 1)

                def rope(name, t, m, dst, cos, sin):
                    s = t % 2
                    ve.wait_ge(free_s[m], uses_before(m, f"{name}{m}", l) + 1)
                    step(tt(rraw[:, s, :], rraw[:, s, :], cos[:, :], ALU.mult))
                    step(tt(rrot[:, s, :], rrot[:, s, :], sin[:, :], ALU.mult))
                    step.settle()
                    tt(dst, rraw[:, s, :], rrot[:, s, :], ALU.add).then_inc(rope_done, 1)

                def qi_out():
                    for m in range(4):
                        rope("qi", m, m, qi[:, m, :], cos_i, sin_i)
                slot(l, "xr", (none, none, qi_out))
                ve.wait_ge(free_s[4], uses_before(4, "kiwi", l) + 1)
                step(tt(rraw[0:64, 0, :], rraw[0:64, 0, :], cos_i[0:64, :], ALU.mult))
                step(tt(rrot[0:64, 0, :], rrot[0:64, 0, :], sin_i[0:64, :], ALU.mult))
                step.settle()
                tt(ki_a[0:32, :], rraw[0:32, 0, :], rrot[0:32, 0, :], ALU.add)
                tt(ki_b[32:64, :], rraw[0:32, 0, :], rrot[0:32, 0, :], ALU.add)
                tt(ki_a[64:96, :], rraw[32:64, 0, :], rrot[32:64, 0, :], ALU.subtract)
                tt(ki_b[96:P, :], rraw[32:64, 0, :], rrot[32:64, 0, :], ALU.subtract).then_inc(rope_done, 1)

                def idx_add(i):
                    if i == 1:
                        ve.wait_ge(free_s[4], uses_before(4, "wi", l) + 1)
                    for h in range(IDX_HEADS):
                        u = IDX.index((i, h))
                        b = 5 + u % 2
                        n = (i + 1) * P
                        ve.wait_ge(free_s[b], uses_before(b, f"idx{u}", l) + 1)
                        if h:
                            ve.wait_ge(idx_acc, l * len(IDX) + (2 + u))
                        stt(acc_of(i), rel[:, u % 2, 0:n], wi[:, i, h:h + 1],
                            acc_of(i) if h else causal[:, (TT - 1 - i) * P:TT * P], ALU.mult, ALU.add).then_inc(idx_acc, 1)

                rounds = [0]
                per = TOPK // 8

                def topk(upto):
                    for r in range(rounds[0], upto):
                        i = 1 + r // per
                        if r % per == 0:
                            ve.wait_ge(idx_acc, l * len(IDX) + (2 + i * IDX_HEADS))
                            ve.sem_inc(dve_step, 1)
                            step.n += 1
                        step.settle()
                        step(v_.max(best[:, :], acc_of(i)))
                        step.settle()
                        step(v_.match_replace(acc_of(i), best[:, :], acc_of(i), TAKEN))
                        if r % per == per - 1:
                            step.settle()
                            step(ts(acc_of(i), acc_of(i), TAKEN, -BIG, ALU.not_equal, ALU.mult))
                    rounds[0] = max(rounds[0], upto)

                def conv(m):
                    if m == 0:
                        step.settle()
                    ve.wait_ge(free_s[m], uses_before(m, f"xr{m}", l) + 1)
                    for j in range(CONV):
                        w = vcol("conv_w", j * LT + m)
                        src = xr[:, m, j:j + T]
                        if j == 0:
                            step(ts(xc[:, m, :], src, w, vcol("conv_b", m), ALU.mult, ALU.add))
                        else:
                            step.settle()
                            ins = stt(xc[:, m, :], src, w, xc[:, m, :], ALU.mult, ALU.add)
                            if j == CONV - 1:
                                ins.then_inc(conv_done, 1)
                            else:
                                step(ins)

                slot(l, "yg", (none, none, none))
                idx_add(1)
                slot(l, "v", (lambda: conv(0), lambda: (conv(1), conv(2)), lambda: conv(3)))
                idx_add(2)

                def lru_input(m):
                    ve.wait_ge(free_s[5], uses_before(5, f"gi{m}", l) + 1)
                    ve.wait_ge(conv_done, l * LT + (m + 1))
                    step(tt(xc[:, m, :], xc[:, m, :], gi[:, m, :], ALU.mult))
                    ve.wait_ge(lru_exp, l * LT + (m + 1))
                    step.settle()
                    step(tt(gi[:, m, :], lru_a[:, m, :], lru_a[:, m, :], ALU.mult))
                    step.settle()
                    stt(th[:, m, :], gi[:, m, :], 1.0, th[:, m, :], ALU.add, ALU.mult).then_inc(lru_m, 1)

                def lru_scan(m):
                    ve.wait_ge(lru_sqrt, l * LT + (m + 1))
                    step(tt(th[:, m, :], th[:, m, :], xc[:, m, :], ALU.mult))
                    step.settle()
                    step(v_.tensor_tensor_scan(gi[:, m, :], lru_a[:, m, :], th[:, m, :], 0.0, ALU.mult, ALU.add))
                    step.settle()
                    tt(xc[:, m, :], gi[:, m, :], yg[:, m, :], ALU.mult).then_inc(lru_out, 1)

                slot(l, "k", (lambda: topk(5), lambda: topk(10), lambda: topk(14)))
                idx_add(3)

                def k_out():
                    for m in range(HEADS):
                        rope("k", 9 + m, m, k[:, m, :], cos_m, sin_m)
                slot(l, "q", (lambda: topk(18), lambda: topk(22), lambda: (topk(24), k_out())))

                def q_out():
                    for m in range(HEADS):
                        rope("q", 13 + m, m, q[:, m, :], cos_m, sin_m)
                slot(l, "out0", (lambda: topk(28), lambda: topk(32), lambda: (topk(34), q_out())))

                def mask_scores(u):
                    i, h = UNITS[u]
                    b = 5 + u % 2
                    n = (i + 1) * P
                    ve.wait_ge(full_s[b], uses_before(b, f"s{u}", l) + 1)
                    if u >= 4:
                        ve.wait_ge(full_s[2 + u % 2], uses_before(2 + u % 2, f"pt{u - 4}", l) + 1)
                    pr = probs[:, u % 4, 0:n]
                    tt(pr, banks[b][:, 0:n], bias_of(i), ALU.add).then_inc(free_s[b], 1)
                    ve.wait_ge(free_s[b], uses_before(b, f"s{u}", l) + 1)
                    step(v_.reduce_max(mx[:, u:u + 1], pr, AX_X))
                    step.settle()
                    ts(negm[:, u:u + 1], mx[:, u:u + 1], -SCALE, None, ALU.mult).then_inc(attn_max, 1)

                def normalize(u):
                    i, h = UNITS[u]
                    ve.wait_ge(attn_exp, l * 16 + (u + 1))
                    step(v_.reciprocal(rinv[:, u:u + 1], rsum[:, u:u + 1]))
                    step.settle()
                    pr = probs[:, u % 4, 0:(i + 1) * P]
                    ts(pr, pr, rinv[:, u:u + 1], None, ALU.mult).then_inc(attn_p, 1)

                for u in range(len(UNITS)):
                    i, h = UNITS[u]
                    if i:
                        topk(i * per)
                        step.settle()
                    mask_scores(u)
                    topk(min(34 + 2 * (u + 1), 3 * per))
                    if u < LT:
                        lru_input(u)
                    elif 7 <= u < 7 + LT:
                        lru_scan(u - 7)
                    if u:
                        normalize(u - 1)
                normalize(len(UNITS) - 1)

                mean_square(l, 4, "lms", LW)
                per_token(l * 4 + 1, diag_l)
                mean_square(l, 5, "ams", AW)
                per_token(l * 4 + 2, diag_a)

                def merged_lo(n):
                    kk = OUT_ORDER[n]
                    ve.wait_ge(b_hi_s, l * (5 * DK) + (n + 1))
                    tt(b_lo[:, kk, :], full[:, n % 2, :], b_hi[:, kk, :].bitcast(F32), ALU.subtract).then_inc(b_lo_s, 1)
                for n, kk in enumerate(OUT_ORDER):
                    if kk >= HEADS:
                        src, g, b, name = xc[:, kk - HEADS, :], vcol("g_lru_out", kk - HEADS), 4, "lrb"
                    else:
                        src, g, b, name = ao[:, kk, :], vcol("g_attn_out", kk), 5, "arb"
                    ve.wait_ge(full_s[b], uses_before(b, name, l) + 1)
                    if n >= 2:
                        ve.wait_ge(b_lo_s, l * (5 * DK) + (n - 1))
                    stt(full[:, n % 2, :], src, g, banks[b][:, :], ALU.mult, ALU.mult).then_inc(m_full, 1)
                    if n % 4 == 3:
                        ve.wait_ge(m_full, l * DK + (n + 2))
                        ve.sem_inc(free_s[b], 1)
                    if n:
                        merged_lo(n - 1)
                merged_lo(DK - 1)

                ve.wait_ge(x_scaled, l * 2 * DK + DK)

                def late_mods():
                    at, _ = VEC["b_mod"]
                    ve.wait_ge(mods_turned, l + 1)
                    tt(mods[:, MODS_NEXT:].rearrange("p (r t) -> p r t", t=TT),
                       banks[7][:, 0:MODS_LATE].rearrange("p (t r) -> p r t", t=TT),
                       vec[:, at + MODS_NEXT:at + 6 * DK].rearrange("p (r t) -> p r t", t=TT), ALU.add).then_inc(mods_out, 1)
                    ve.wait_ge(mods_out, l * (NC + 1) + 2)
                    for gate in (2, 5):
                        step(ts(mods[:, gate * DK:(gate + 1) * DK], mods[:, gate * DK:(gate + 1) * DK], 1.0, None, ALU.add))
                    fold_gains(1, mods[:, 3 * DK:4 * DK], mods[:, 4 * DK:5 * DK], vcol("ln1_g", 0, DK), vcol("ln1_b", 0, DK))

                def out_out(j):
                    def run():
                        for m in range(4 * j, 4 * j + 4):
                            residual(l, f"out{j}", m, 2)
                            ln_sum(l, f"out{j}", m)
                    return run
                slot(l, "out1", (none, none, lambda: (late_mods(), out_out(0)())))
                slot(l, "up0", (none, none, out_out(1)), nc_=0)
                ln_stats(l, "", l * 4 + 3)
                norm_tile(0)
                for kk in range(1, DK):
                    norm_tile(kk)
                    a_lo_tile(l, 1, kk - 1)
                a_lo_tile(l, 1, DK - 1)
                step.restart()

                def chunk(l, c, last):
                    def hidden(j):
                        b0 = l * (5 * DK) + c * DK + DK

                        def lo(t):
                            ve.wait_ge(b_hi_s, b0 + (t + 1))
                            tt(b_lo[:, t, :], ffsq[:, t % 2, :], b_hi[:, t, :].bitcast(F32), ALU.subtract).then_inc(b_lo_s, 1)

                        def run():
                            for m in range(4):
                                t = 4 * j + m
                                b = bank_set(f"up{j}") + m
                                ve.wait_ge(free_s[b], uses_before(b, f"up{j}{m}", l, c) + 1)
                                ve.wait_ge(b_hi_s, b0 + t - 1)
                                ve.wait_ge(b_lo_s, b0 + t - 1)
                                tt(ffsq[:, t % 2, :], relu[:, t % 2, :], relu[:, t % 2, :], ALU.mult).then_inc(ff_sq, 1)
                                if m:
                                    lo(t - 1)
                            lo(4 * j + 3)
                        return run

                    def down_out(j):
                        def run():
                            for m in range(4 * j, 4 * j + 4):
                                residual(l, f"down{j}", m, 5, c)
                                if last:
                                    ln_sum(l, f"down{j}", m, c)
                        return run
                    def weigh_next(n):
                        def run():
                            ve.wait_ge(mod_in[n], l * (16 * MOD_PAIRS // MR) + c * 16 + (16 * LATE_PAIRS // MR + 16))
                            weigh(mod_raw[:, n, :, :])
                        return run
                    def next_mods():
                        ve.wait_ge(mod_used, l * MOD_PAIRS + c * 2 + (NEXT_PAIRS + LATE_PAIRS + 2))
                        v_.tensor_copy(modn[:, bass.ds(c * TT, TT)], banks[7][:, 0:TT]).then_inc(mods_out, 1)
                    slot(l, "up1", (weigh_next(0), weigh_next(1), lambda: (next_mods(), hidden(0)())), c)
                    if not last:
                        slot(l, "down0", (none, none, hidden(1)), c)
                        ve.wait_ge(x_scaled, (l + 1) * 2 * DK)
                        slot(l, "down1", (none, none, down_out(0)), c)
                        slot(l, "up0", (none, none, down_out(1)), c + 1)
                    else:
                        slot(l, "down0", (none, none, hidden(1)), c)
                        slot(l, "down1", (none, none, down_out(0)), c)
                        ve.wait_ge(mods_out, (l + 1) * (NC + 1) + 1)
                        next_gains((l + 1) % DEPTH, vcol("ln2_g", 0, DK), vcol("ln2_b", 0, DK))
                        down_out(1)()
                    step.restart()
                chunks(ve, l, chunk)
                ln_stats(l, "_b", l * 4 + 4)
                step.restart()
            layers(ve, layer)
            for kk in range(DK):
                norm_tile(kk)


ROUND = 1.5 * 2.0 ** 23
TWO_PI = (6.28125, 0.001934051513671875, 2 * np.pi - 6.28125 - 0.001934051513671875)
PI_IN = 3.1415925

INS = ["x", "c", "positions", "w_mod", "b_mod", "w_in", "conv_w", "conv_b", "w_gate_a", "b_gate_a", "w_gate_x",
       "b_gate_x", "lru_lambda", "g_attn_out", "g_lru_out", "w_out", "ln1_g", "ln1_b", "w_up", "w_down", "ln2_g", "ln2_b"]


def rope_frequencies():
    out = np.zeros((P, 2), np.float32)
    for col, (dim, per) in enumerate(((DH, 64), (IDX_DH, 32))):
        inv = np.float32(THETA) ** (-np.arange(0, dim, 2, dtype=np.float32) / np.float32(dim))
        p = np.arange(P)
        out[:, col] = inv[p % per] * np.where(p < 64, -1, 1)
    return out


def kernel(**inputs):
    import concourse.bacc as bacc
    from concourse.bass_utils import run_bass_kernel_spmd

    nc = bacc.Bacc("TRN2", target_bir_lowering=False, num_devices=1)
    arrays, args = {}, {}
    for name, a in [(n, inputs[n]) for n in INS] + [("freq", rope_frequencies())]:
        a = np.ascontiguousarray(a)
        arrays[f"in_{name}_dram"] = a
        args[name] = nc.dram_tensor(f"in_{name}_dram", a.shape, mybir.dt.from_np(a.dtype), kind="ExternalInput").ap()
    out = nc.dram_tensor("out_dram", (1, T, D), F32, kind="ExternalOutput").ap()
    trunk_kernel(nc, args, out)
    r = run_bass_kernel_spmd(nc, [arrays], core_ids=[0])
    return r.results[0]["out_dram"]
```
